# Optimizing a Trainium2 kernel written in Bass

```python
import jax, jax.numpy as jnp
from jax import lax
import numpy as np

D_MODEL = 1024
BATCH = 1
SEQ = 512
DEPTH = 2
DEC_BATCH = 8
DEC_SEQ = 1
PAST_LEN = 1024
PAGE_SIZE = 128

N_A_LAYERS = DEPTH // 2
N_B_LAYERS = DEPTH - N_A_LAYERS
RET_HEADS = 4
RET_DK = D_MODEL // RET_HEADS
RET_DV = D_MODEL // RET_HEADS
RET_CHUNK = 128
MLA_HEADS = 8
QK_NOPE = D_MODEL // MLA_HEADS
QK_ROPE = 64
V_HEAD = D_MODEL // MLA_HEADS
Q_LORA = D_MODEL // 4
KV_LORA = D_MODEL // 4
MLA_BLOCK_Q = 128
MLA_SCALE = (QK_NOPE + QK_ROPE) ** -0.5
N_EXPERTS = 16
N_GROUPS = 4
EXPERTS_PER_GROUP = N_EXPERTS // N_GROUPS
TOP_K = 2
D_EXPERT = D_MODEL // 2

ROPE_THETA = 10000.0
EPS = 1e-6
NEG = -1e30

kernel_name = "yoco_retention_mla_grouped_moe_step"

def rmsnorm(x, g):
    xf = x.astype(jnp.float32)
    y = xf * lax.rsqrt(jnp.mean(xf * xf, axis=-1, keepdims=True) + EPS)
    return (y * g.astype(jnp.float32)).astype(x.dtype)

def modulate(h, shift, scale):
    return h * (1 + scale[:, None, :]) + shift[:, None, :]

def rope(x, pos):
    d = x.shape[-1]
    inv = ROPE_THETA ** (-jnp.arange(0, d, 2, dtype=jnp.float32) / d)
    ang = pos.astype(jnp.float32)[:, None] * inv[None, :]
    cos = jnp.cos(ang)[None, :, None, :]
    sin = jnp.sin(ang)[None, :, None, :]
    xf = x.astype(jnp.float32)
    x1, x2 = xf[..., : d // 2], xf[..., d // 2:]
    return jnp.concatenate([x1 * cos - x2 * sin, x1 * sin + x2 * cos], axis=-1).astype(x.dtype)

def retention_log_decay():
    return jnp.log1p(-jnp.exp2(-5.0 - jnp.arange(RET_HEADS, dtype=jnp.float32)))

def retention_chunk(q, k, v, S, log_g):
    L = q.shape[1]
    idx = jnp.arange(L, dtype=jnp.float32)
    diff = idx[:, None] - idx[None, :]
    decay = jnp.where(diff[None] >= 0, jnp.exp(jnp.maximum(diff, 0.0)[None] * log_g[:, None, None]), 0.0)
    scores = jnp.einsum('blhd,bmhd->bhlm', q, k) * decay[None]
    inner = jnp.einsum('bhlm,bmhv->blhv', scores, v)
    q_decay = jnp.exp((idx + 1.0)[:, None] * log_g[None, :])
    cross = jnp.einsum('blhd,bhdv->blhv', q * q_decay[None, :, :, None], S)
    k_decay = jnp.exp((L - 1.0 - idx)[:, None] * log_g[None, :])
    S_new = jnp.exp(L * log_g)[None, :, None, None] * S + jnp.einsum('blhd,blhv->bhdv', k * k_decay[None, :, :, None], v)
    return inner + cross, S_new

def retention_prompt(q, k, v, log_g):
    B, S, H, dk = q.shape
    dv = v.shape[-1]
    nc = S // RET_CHUNK
    resh = lambda t: t.reshape(B, nc, RET_CHUNK, H, t.shape[-1]).swapaxes(0, 1)
    S0 = jnp.zeros((B, H, dk, dv), jnp.float32)

    def step(state, qkv):
        o, state = retention_chunk(qkv[0], qkv[1], qkv[2], state, log_g)
        return state, o

    S_fin, o = lax.scan(step, S0, (resh(q), resh(k), resh(v)))
    return o.swapaxes(0, 1).reshape(B, S, H, dv), S_fin

def retention_mixer(h, pos, state, w_in, gn_g, w_out):
    B, S, _ = h.shape
    nqk = RET_HEADS * RET_DK
    nv = RET_HEADS * RET_DV
    proj = h @ w_in
    q = proj[..., :nqk].reshape(B, S, RET_HEADS, RET_DK)
    k = proj[..., nqk:2 * nqk].reshape(B, S, RET_HEADS, RET_DK)
    v = proj[..., 2 * nqk:2 * nqk + nv].reshape(B, S, RET_HEADS, RET_DV).astype(jnp.float32)
    g = proj[..., 2 * nqk + nv:]
    q = rope(q, pos).astype(jnp.float32) * (RET_DK ** -0.5)
    k = rope(k, pos).astype(jnp.float32)
    log_g = retention_log_decay()
    if state is None:
        o, s_new = retention_prompt(q, k, v, log_g)
    else:
        o, s_new = retention_chunk(q, k, v, state.astype(jnp.float32), log_g)
    mu = jnp.mean(o, axis=-1, keepdims=True)
    var = jnp.mean(jnp.square(o - mu), axis=-1, keepdims=True)
    o = ((o - mu) * lax.rsqrt(var + EPS)).reshape(B, S, nv) * gn_g.astype(jnp.float32)
    y = (jax.nn.silu(g.astype(jnp.float32)) * o).astype(h.dtype) @ w_out
    return y, s_new

def mla_kv_stream(x, c_silu, pos, kv_w_ada, kv_b_ada, kv_norm_g, w_dkv, kv_latent_norm_g):
    shift, scale = jnp.split(c_silu @ kv_w_ada + kv_b_ada, 2, axis=-1)
    hn = modulate(rmsnorm(x, kv_norm_g), shift, scale)
    z = hn @ w_dkv
    ckv = rmsnorm(z[..., :KV_LORA], kv_latent_norm_g)
    kpe = rope(z[..., KV_LORA:][:, :, None, :], pos)[:, :, 0, :]
    return ckv, kpe

def mla_query(h, pos, w_dq, q_norm_g, w_uq, w_uk):
    B, S, _ = h.shape
    cq = rmsnorm(h @ w_dq, q_norm_g)
    q = (cq @ w_uq).reshape(B, S, MLA_HEADS, QK_NOPE + QK_ROPE)
    q_nope, q_pe = q[..., :QK_NOPE], q[..., QK_NOPE:]
    q_pe = rope(q_pe, pos)
    q_lat = jnp.einsum('bshn,hnc->bshc', q_nope, w_uk)
    return q_lat, q_pe

def mla_out(o_lat, w_uv, w_o):
    o = jnp.einsum('bqhc,hvc->bqhv', o_lat, w_uv)
    B, S = o.shape[:2]
    return o.reshape(B, S, MLA_HEADS * V_HEAD) @ w_o

def mla_attend_prompt(q_lat, q_pe, ckv, kpe):
    B, S, H, C = q_lat.shape
    nb = S // MLA_BLOCK_Q
    kpos = jnp.arange(S)

    def block(args):
        ql, qp, i = args
        s = (jnp.einsum('bqhc,bkc->bhqk', ql, ckv) + jnp.einsum('bqhr,bkr->bhqk', qp, kpe)).astype(jnp.float32) * MLA_SCALE
        qpos = i * MLA_BLOCK_Q + jnp.arange(MLA_BLOCK_Q)
        s = jnp.where((kpos[None, :] <= qpos[:, None])[None, None], s, NEG)
        p = jax.nn.softmax(s, axis=-1).astype(ckv.dtype)
        return jnp.einsum('bhqk,bkc->bqhc', p, ckv)

    ql_b = q_lat.reshape(B, nb, MLA_BLOCK_Q, H, C).swapaxes(0, 1)
    qp_b = q_pe.reshape(B, nb, MLA_BLOCK_Q, H, QK_ROPE).swapaxes(0, 1)
    o = lax.map(block, (ql_b, qp_b, jnp.arange(nb)))
    return o.swapaxes(0, 1).reshape(B, S, H, C)

def mla_attend_sample(q_lat, q_pe, past_ckv, past_kpe, new_ckv, new_kpe):
    L = new_ckv.shape[1]
    P = past_ckv.shape[1]
    s_past = jnp.einsum('bqhc,bkc->bhqk', q_lat, past_ckv) + jnp.einsum('bqhr,bkr->bhqk', q_pe, past_kpe)
    s_new = jnp.einsum('bqhc,bkc->bhqk', q_lat, new_ckv) + jnp.einsum('bqhr,bkr->bhqk', q_pe, new_kpe)
    causal = jnp.arange(L)[None, :] <= jnp.arange(L)[:, None]
    s_new = jnp.where(causal[None, None], s_new.astype(jnp.float32) * MLA_SCALE, NEG)
    s = jnp.concatenate([s_past.astype(jnp.float32) * MLA_SCALE, s_new], axis=-1)
    p = jax.nn.softmax(s, axis=-1).astype(new_ckv.dtype)
    return (jnp.einsum('bhqk,bkc->bqhc', p[..., :P], past_ckv)
            + jnp.einsum('bhqk,bkc->bqhc', p[..., P:], new_ckv))

def moe_ffn(h, router_w, router_bias, w_gate, w_up, w_down, ws_gate, ws_up, ws_down):
    B, S, D = h.shape
    t = h.reshape(B * S, D)
    scores = jax.nn.sigmoid((t @ router_w).astype(jnp.float32))
    sel = (scores + router_bias.astype(jnp.float32)).reshape(-1, N_GROUPS, EXPERTS_PER_GROUP)
    group_score = jnp.sum(lax.top_k(sel, TOP_K)[0], axis=-1)
    best = jnp.argmax(group_score, axis=-1)
    in_group = best[:, None] == jnp.arange(N_GROUPS)[None, :]
    masked = jnp.where(in_group[..., None], sel, -jnp.inf).reshape(-1, N_EXPERTS)
    _, top_idx = lax.top_k(masked, TOP_K)
    top_s = jnp.take_along_axis(scores, top_idx, axis=-1)
    wts = top_s / jnp.sum(top_s, axis=-1, keepdims=True)
    gates = jnp.sum(jax.nn.one_hot(top_idx, N_EXPERTS, dtype=jnp.float32) * wts[..., None], axis=1)
    hid = jax.nn.silu(jnp.einsum('td,edf->tef', t, w_gate)) * jnp.einsum('td,edf->tef', t, w_up)
    hid = hid * gates.astype(hid.dtype)[..., None]
    routed = jnp.einsum('tef,efd->td', hid, w_down)
    shared = (jax.nn.silu(t @ ws_gate) * (t @ ws_up)) @ ws_down
    return (routed + shared).reshape(B, S, D)

def run_trunk(x, c, pos, ret_state, attend, P):
    c_silu = jax.nn.silu(c)
    new_ret = []
    ckv = kpe = None
    for l in range(DEPTH):
        mod = c_silu @ P['w_ada'][l] + P['b_ada'][l]
        sh1, sc1, g1, sh2, sc2, g2 = jnp.split(mod, 6, axis=-1)
        if l == N_A_LAYERS:
            ckv, kpe = mla_kv_stream(x, c_silu, pos, P['kv_w_ada'], P['kv_b_ada'], P['kv_norm_g'],
                                     P['mla_w_dkv'], P['mla_kv_norm_g'])
        h = modulate(rmsnorm(x, P['norm_mix_g'][l]), sh1, sc1)
        if l < N_A_LAYERS:
            st = None if ret_state is None else ret_state[l]
            y, s_new = retention_mixer(h, pos, st, P['ret_w_in'][l], P['ret_gn_g'][l], P['ret_w_out'][l])
            new_ret.append(s_new)
        else:
            j = l - N_A_LAYERS
            q_lat, q_pe = mla_query(h, pos, P['mla_w_dq'][j], P['mla_q_norm_g'][j], P['mla_w_uq'][j], P['mla_w_uk'])
            y = mla_out(attend(q_lat, q_pe, ckv, kpe), P['mla_w_uv'], P['mla_w_o'][j])
        x = x + g1[:, None, :] * y
        h = modulate(rmsnorm(x, P['norm_ffn_g'][l]), sh2, sc2)
        x = x + g2[:, None, :] * moe_ffn(h, P['router_w'], P['router_bias'], P['moe_w_gate'][l], P['moe_w_up'][l],
                                         P['moe_w_down'][l], P['shared_w_gate'][l], P['shared_w_up'][l], P['shared_w_down'][l])
    return rmsnorm(x, P['final_norm_g']), jnp.stack(new_ret), ckv, kpe

def setup_inputs(seed: int = 0) -> dict:
    key = jax.random.key(seed)
    ks = iter(jax.random.split(key, 48))
    f32 = jnp.float32

    def nrm(shape, scale):
        return jax.random.normal(next(ks), shape, f32) * scale

    def gain(shape):
        return 1.0 + nrm(shape, 0.01)

    n_pages = PAST_LEN // PAGE_SIZE
    n_used = DEC_BATCH * n_pages
    n_phys = n_used + n_used // 4
    D = D_MODEL
    ret_cols = RET_HEADS * (2 * RET_DK + 2 * RET_DV)
    perm = jax.random.permutation(next(ks), n_phys)
    return {
        'x_prompt': nrm((BATCH, SEQ, D), 1.0),
        'x_sample': nrm((DEC_BATCH, DEC_SEQ, D), 1.0),
        'c_prompt': nrm((BATCH, D), 1.0),
        'c_sample': nrm((DEC_BATCH, D), 1.0),
        'state_ret': nrm((N_A_LAYERS, DEC_BATCH, RET_HEADS, RET_DK, RET_DV), 4.0),
        'cache_ckv': nrm((n_phys, PAGE_SIZE, KV_LORA), 1.0),
        'cache_kpe': nrm((n_phys, PAGE_SIZE, QK_ROPE), 1.0),
        'page_table': perm[:n_used].reshape(DEC_BATCH, n_pages).astype(jnp.int32),
        'w_ada': nrm((DEPTH, D, 6 * D), 0.5 * D ** -0.5),
        'b_ada': nrm((DEPTH, 6 * D), 0.02),
        'norm_mix_g': gain((DEPTH, D)),
        'norm_ffn_g': gain((DEPTH, D)),
        'ret_w_in': nrm((N_A_LAYERS, D, ret_cols), D ** -0.5),
        'ret_gn_g': gain((N_A_LAYERS, RET_HEADS * RET_DV)),
        'ret_w_out': nrm((N_A_LAYERS, RET_HEADS * RET_DV, D), (RET_HEADS * RET_DV) ** -0.5),
        'kv_w_ada': nrm((D, 2 * D), 0.5 * D ** -0.5),
        'kv_b_ada': nrm((2 * D,), 0.02),
        'kv_norm_g': gain((D,)),
        'mla_w_dkv': nrm((D, KV_LORA + QK_ROPE), D ** -0.5),
        'mla_kv_norm_g': gain((KV_LORA,)),
        'mla_w_uk': nrm((MLA_HEADS, QK_NOPE, KV_LORA), KV_LORA ** -0.5),
        'mla_w_uv': nrm((MLA_HEADS, V_HEAD, KV_LORA), KV_LORA ** -0.5),
        'mla_w_dq': nrm((N_B_LAYERS, D, Q_LORA), D ** -0.5),
        'mla_q_norm_g': gain((N_B_LAYERS, Q_LORA)),
        'mla_w_uq': nrm((N_B_LAYERS, Q_LORA, MLA_HEADS * (QK_NOPE + QK_ROPE)), Q_LORA ** -0.5),
        'mla_w_o': nrm((N_B_LAYERS, MLA_HEADS * V_HEAD, D), (MLA_HEADS * V_HEAD) ** -0.5),
        'router_w': nrm((D, N_EXPERTS), D ** -0.5),
        'router_bias': nrm((N_EXPERTS,), 0.01),
        'moe_w_gate': nrm((DEPTH, N_EXPERTS, D, D_EXPERT), D ** -0.5),
        'moe_w_up': nrm((DEPTH, N_EXPERTS, D, D_EXPERT), D ** -0.5),
        'moe_w_down': nrm((DEPTH, N_EXPERTS, D_EXPERT, D), D_EXPERT ** -0.5),
        'shared_w_gate': nrm((DEPTH, D, D_EXPERT), D ** -0.5),
        'shared_w_up': nrm((DEPTH, D, D_EXPERT), D ** -0.5),
        'shared_w_down': nrm((DEPTH, D_EXPERT, D), D_EXPERT ** -0.5),
        'final_norm_g': gain((D,)),
    }

def reference(x_prompt, x_sample, c_prompt, c_sample, state_ret, cache_ckv, cache_kpe, page_table,
              w_ada, b_ada, norm_mix_g, norm_ffn_g, ret_w_in, ret_gn_g, ret_w_out,
              kv_w_ada, kv_b_ada, kv_norm_g, mla_w_dkv, mla_kv_norm_g, mla_w_uk, mla_w_uv,
              mla_w_dq, mla_q_norm_g, mla_w_uq, mla_w_o, router_w, router_bias,
              moe_w_gate, moe_w_up, moe_w_down, shared_w_gate, shared_w_up, shared_w_down, final_norm_g):
    P = {
        'w_ada': w_ada, 'b_ada': b_ada, 'norm_mix_g': norm_mix_g, 'norm_ffn_g': norm_ffn_g,
        'ret_w_in': ret_w_in, 'ret_gn_g': ret_gn_g, 'ret_w_out': ret_w_out,
        'kv_w_ada': kv_w_ada, 'kv_b_ada': kv_b_ada, 'kv_norm_g': kv_norm_g,
        'mla_w_dkv': mla_w_dkv, 'mla_kv_norm_g': mla_kv_norm_g, 'mla_w_uk': mla_w_uk, 'mla_w_uv': mla_w_uv,
        'mla_w_dq': mla_w_dq, 'mla_q_norm_g': mla_q_norm_g, 'mla_w_uq': mla_w_uq, 'mla_w_o': mla_w_o,
        'router_w': router_w, 'router_bias': router_bias,
        'moe_w_gate': moe_w_gate, 'moe_w_up': moe_w_up, 'moe_w_down': moe_w_down,
        'shared_w_gate': shared_w_gate, 'shared_w_up': shared_w_up, 'shared_w_down': shared_w_down,
        'final_norm_g': final_norm_g,
    }
    pos_p = jnp.arange(x_prompt.shape[1])
    y_prompt, state_ret_prompt, ckv_prompt, kpe_prompt = run_trunk(x_prompt, c_prompt, pos_p, None, mla_attend_prompt, P)

    n_seq, n_pages = page_table.shape
    past_len = n_pages * cache_ckv.shape[1]
    past_ckv = cache_ckv[page_table].reshape(n_seq, past_len, KV_LORA)
    past_kpe = cache_kpe[page_table].reshape(n_seq, past_len, QK_ROPE)
    pos_s = past_len + jnp.arange(x_sample.shape[1])

    def attend_sample(q_lat, q_pe, new_ckv, new_kpe):
        return mla_attend_sample(q_lat, q_pe, past_ckv, past_kpe, new_ckv, new_kpe)

    y_sample, state_ret_sample, ckv_sample, kpe_sample = run_trunk(x_sample, c_sample, pos_s, state_ret, attend_sample, P)
    return (y_prompt, y_sample, state_ret_prompt, state_ret_sample, ckv_prompt, kpe_prompt, ckv_sample, kpe_sample)


_drawn_inputs = setup_inputs


def setup_inputs(seed=0):
    import zlib

    import numpy as np

    out = dict(_drawn_inputs(seed))
    spreads = {}
    factors = {'cache_ckv': 3.774,
     'cache_kpe': 7.33,
     'norm_mix_g': 3.409,
     'norm_ffn_g': 2.86,
     'ret_gn_g': 4.514,
     'kv_norm_g': 5.955,
     'mla_kv_norm_g': 5.707,
     'mla_q_norm_g': 8.0,
     'final_norm_g': 5.696}
    for name, (base, spread) in spreads.items():
        noise = np.random.default_rng([zlib.crc32(name.encode()), seed]).standard_normal(out[name].shape)
        drawn = base * np.exp(spread * noise) if base else spread * noise
        out[name] = __import__('jax').numpy.asarray(drawn.astype(out[name].dtype))
    for name, factor in factors.items():
        out[name] = (out[name] * factor).astype(out[name].dtype)
    return out
```

```python
from contextlib import ExitStack

import numpy as np

import concourse.bass as bass
from concourse import mybir

F32 = mybir.dt.float32
I32 = mybir.dt.int32
ALU = mybir.AluOpType
ACT = mybir.ActivationFunctionType
AX = mybir.AxisListType

P = 128
D = 1024
DT = D // P
NP, NS = 512, 8
HALF, HP, HS = 260, 256, 4
T = NP + NS
PAST = 1024
RH, RD = 4, 256
MH, NOPE, ROPE, LAT = 8, 128, 64, 256
NE, NG, EG = 16, 4, 4
FE = 512
FT = FE // P
PAGE, NPAGE = 128, 8
MLA_SCALE = (NOPE + ROPE) ** -0.5
EPS = 1e-6
NSEQ = 1 + NS
ADA_UNITS = 28
MAXBLK = NE + 2 * T // P
TABLE = MAXBLK + 2
MAIN = P

WIDTHS = [("ident", P), ("ones", P), ("inv256", P), ("tri", P), ("decay", RH * NP), ("kdec", RH * 4),
          ("cosr", 2 * HALF), ("sinr", 2 * HALF), ("cosm", 2 * HALF), ("sinm", 2 * HALF), ("rot", ROPE),
          ("causal", P), ("rev16", NE), ("iota16", NE), ("rev4", NG), ("valid", 5), ("tokid", 5),
          ("eps", 1), ("iota8", 8), ("selq", 2 * P)]
AT, _at = {}, 0
for _n, _w in WIDTHS:
    AT[_n] = (_at, _w)
    _at += _w
CW = _at

G_MIX, G_FFN, G_KV, G_GN, G_FIN, G_CKV, G_CQ, N_GAIN = 0, 16, 32, 40, 48, 56, 58, 60
N_BIAS = 112


def shape_tables():
    c = np.zeros((P, CW), np.float32)

    def put(name, a):
        s, w = AT[name]
        a = np.asarray(a, np.float32).reshape(-1, w)
        c[:a.shape[0], s:s + w] = a

    p = np.arange(P)
    put("ident", np.eye(P))
    put("ones", np.ones((P, P)))
    put("inv256", np.full((P, P), 1 / RD))
    put("tri", p[:, None] < p[None, :])
    g = 1 - np.exp2(-5.0 - np.arange(RH))
    x = np.arange(NP)
    diff = x[None, None, :] - p[:, None, None]
    put("decay", np.where(diff >= 0, g[None, :, None] ** np.maximum(diff, 0), 0) * RD ** -0.5)
    put("kdec", g[None, :, None] ** (NP - 1 - (P * np.arange(4)[None, None, :] + p[:, None, None])))
    half = np.zeros((2, HALF))
    half[:, :HP] = np.arange(NP).reshape(2, HP)
    half[:, HP:] = PAST
    pos = half.reshape(-1).astype(np.float32)
    for name, d in (("r", RD), ("m", ROPE)):
        inv = np.float32(10000.0) ** (-np.arange(0, d, 2, dtype=np.float32) / np.float32(d))
        if d == ROPE:
            inv = np.tile(inv, 2)
        ang = (pos[None, :] * inv[:, None].astype(np.float32)).astype(np.float64)
        put("cos" + name, np.cos(ang))
        put("sin" + name, np.sin(ang))
    rot = np.zeros((ROPE, ROPE))
    q = np.arange(ROPE // 2)
    rot[q + 32, q] = -1
    rot[q, q + 32] = 1
    put("rot", rot)
    put("causal", np.where(p[None, :] <= p[:, None], 0, -1e30))
    put("rev16", np.tile(NE - np.arange(NE), (P, 1)))
    put("iota16", np.tile(np.arange(NE), (P, 1)))
    put("rev4", np.tile(NG - np.arange(NG), (P, 1)))
    put("valid", np.stack([np.ones(P)] * 4 + [p < NS], 1))
    put("tokid", np.stack([P * i + p for i in range(4)] + [NP + np.minimum(p, NS - 1)], 1))
    put("eps", np.full((P, 1), EPS))
    put("iota8", np.tile(np.arange(8), (P, 1)))
    put("selq", p[:NS, None, None] == 4 * np.arange(2)[None, :, None] + p[None, None, :] // 32)
    return c


def build(nc, A, O):
    ctx = ExitStack()
    with ctx:
        def sb(name, shape, dt=F32):
            return ctx.enter_context(nc.sbuf_tensor(name, shape, dt))

        def sem(name):
            return ctx.enter_context(nc.semaphore(name))

        C = sb("shape_tables_sb", [P, CW])
        xT = sb("xT", [P, DT, 2, HALF])
        hT = sb("hT", [P, DT, 2, HALF])
        hS = sb("h_samples", [P, DT, NS])
        W = sb("wring", [P, 6, 4096])
        mod = sb("mod", [P, N_BIAS, NSEQ])
        cols = sb("cols", [P, N_BIAS + N_GAIN])
        csT = sb("csT", [P, DT, 32])
        apart = sb("apart", [P, 2, T])
        asum = sb("asum", [P, 2, 4 * NSEQ])
        acol = sb("acol", [P, DT, NSEQ])
        rs = sb("rs", [P, 2, HALF])
        rw = sb("rw", [P, DT, 32])
        rbias = sb("rbias", [P, NE])
        tmp8 = sb("tmp8", [P, DT, 2, HS])
        niter = sb("niter", [1, 1], I32)
        bexp = sb("bexp", [1, MAXBLK], I32)
        didx = sb("didx", [P, 2, 5], I32)
        idx = sb("idx", [P, TABLE], I32)
        idxc = sb("idxc", [P, 2], I32)
        ptab = sb("ptab", [1, NS * NPAGE], I32)
        AR = 11450
        arena = sb("arena", [P, AR])
        PS = ctx.enter_context(nc.psum_tensor("PS", [P, 8, 512], F32))

        def cst(name):
            s, w = AT[name]
            return C[:, s:s + w]

        ident, ones, inv256, tri = cst("ident"), cst("ones"), cst("inv256"), cst("tri")
        decay = cst("decay").rearrange("p (h x) -> p h x", h=RH)
        two = lambda a: a.rearrange("p (a b) -> p a b", a=2)
        cosr, sinr, cosm, sinm = (two(cst(n)) for n in ("cosr", "sinr", "cosm", "sinm"))

        class Carve:
            def __init__(self, region, at=0):
                self.region, self.at = region, at

            def __call__(self, *shape):
                n = int(np.prod(shape))
                v = self.region[:, self.at:self.at + n]
                self.at += n
                assert self.at <= self.region.shape[1], self.at
                if len(shape) == 2:
                    v = v.rearrange("p (a b) -> p a b", a=shape[0])
                if len(shape) == 3:
                    v = v.rearrange("p (a b c) -> p a b c", a=shape[0], b=shape[1])
                return v

        c0 = Carve(arena[:, :])
        xrows = c0(5, D)
        crow, csilu = c0(D), c0(D)
        brows, grows = c0(P), c0(P)
        rbrow = c0(NE)
        c1 = Carve(arena[:, :])
        qT, kT = c1(2, T), c1(2, T)
        gT = c1(2, 2, HALF)
        vtok = c1(5, RD)
        PT = [c1(NP - P * j) for j in range(4)]
        kdec = c1(4, RD)
        oT = c1(2, T)
        sq = c1(2, T)
        yT = sq.rearrange("p a b -> p (a b)").rearrange("p (a h b) -> p a h b", a=2, h=2)
        rope_at = c1.at
        rt = [c1(2, HALF) for _ in range(4)]
        kmask = Carve(arena[:, :], rope_at)(NS, RD)
        stout = c1(2, RD)
        ks = Carve(sq.rearrange("p a b -> p (a b)"))(RD)
        osb = Carve(arena[:, :], rope_at)(2, RD)
        rs2 = rs[:, :, :]
        ztile = stout.rearrange("p a b -> p (a b)")
        c2 = Carve(arena[:, :])
        hblk = [c2(D) for _ in range(2)]
        hbT = [c2(DT, P) for _ in range(2)]
        ysb = [c2(D) for _ in range(2)]
        sg = c2(FE)
        sgs_at = c2.at
        hid, hidT = c2(FE), c2(FT, P)
        sgs = Carve(arena[:, :], sgs_at)(2, HALF)
        shT = c2(FT, 2, HALF)
        R = {n: c2(5, NE) for n in "sc sel oh1 oh2 a b M pos slot t".split()}
        R4 = {n: c2(5, NG) for n in "top1 m2 l2 gs e4 c4 ing inb".split()}
        hi, lo = c2(40), c2(40)
        lg, lgs = Carve(arena[:, :], sgs_at)(2, HALF), c2(NS)
        R5 = {n: c2(5) for n in "v1 m s1 s2 w1 w2 dsum".split()}
        cnt, ov, ova, ovb, dlt, base16 = (c2(NE) for _ in range(6))
        cmp8 = c2(8, NE)
        nb8 = c2(8)
        bex = c2(MAXBLK)
        nit = c2(4)
        tabz, tabr = c2(P), c2(P)
        c3 = Carve(arena[:, :])
        ckvT = c3(2, T)
        kpeT = apart[:, 0, :]
        ctok = c3(5, LAT + ROPE)
        cqT = c3(2, 2, HALF)
        uvT = c3(MH, 2, P)
        qsl = c3(3, NS, 32)
        share_at = c3.at
        zT = c3(2, 2, HALF)
        zk = c3(2, HALF)
        qn = c3(2, HALF)
        qpr = c3(2, HALF)
        ql = c3(2, T)
        qpe = apart[:, 1, :]
        pr_ = c3(10 * P)
        mcol = c3(16)
        msq = Carve(arena[:, :], share_at + 4 * 2 * HALF)(2, 2, HALF)
        mt = [qn, Carve(pr_)(2, HALF)]
        qt = [zT[:, t, :, :] for t in range(2)]
        dead = C[:, AT["decay"][0]:AT["decay"][0] + 3104]
        c4 = Carve(dead)
        PTm = c4(4, NP)
        olat = c4(2, NP)
        KT = Carve(dead)(3, NPAGE * PAGE)
        c5 = Carve(arena[:, :], share_at)
        S_sb = c5(PAST + 1)
        Ps = c5(PAST + 1)
        PTs = c5(NPAGE, P)
        prodn = c5(3, P)
        onew, olr = c5(LAT), c5(LAT)
        osl = c5(2, NS, MH)
        mcol2 = c5(4)
        TRI = [P * i * (i + 1) // 2 for i in range(5)]
        SCORES = (("sa", ((0, 0), (1, P), (2, 512))), ("sb", ((3, 0),)))
        SCORES = tuple((n + "_mla", c) for n, c in SCORES)
        TURNS = (("pta", ((0, 0), (1, P), (2, 3 * P))), ("ptb", ((3, 0),)))
        orow = [Carve(arena[:, :], 0)(D), Carve(arena[:, :], D)(D)]

        h_dram = [nc.dram_tensor(f"h_rows{l}", (T, D), F32, kind="Internal").ap() for l in range(2)]
        y_dram = nc.dram_tensor("y_rows", (MAXBLK * P, D), F32, kind="Internal").ap()
        t_dram = [nc.dram_tensor(f"slot_table{l}", (TABLE * P, 1), F32, kind="Internal").ap() for l in range(2)]

        s_tab, s_rows, s_c, s_x, s_rw = (sem(n) for n in ("tables_in", "rows_in", "c_in", "x_in", "router_in"))
        s_pt, s_rb = sem("page_table_in"), sem("router_bias_in")
        slot_in = [sem(f"slot_in{i}") for i in range(6)]
        group_done = sem("group_done")
        took = {"dve": sem("dve_took_group"), "act": sem("act_took_group")}
        dve_chain = sem("dve_chain")
        cs_zeroed, rw_zeroed, ada_ready = sem("cs_zeroed"), sem("rw_zeroed"), sem("ada_ready")
        csilu_ready, x_updated = sem("csilu_ready"), sem("x_updated")
        sq_ready, h_scaled, h_ready, hs_ready = (
            sem(n) for n in ("squares_ready", "h_scaled", "h_ready", "h_sample_ready"))
        q_ready, k_ready, km_ready, st_updated, o_ready, oc_ready, osq_ready, y_ready = (
            sem(n) for n in ("q_ready", "k_ready", "kmask_ready", "states_updated", "o_ready", "o_centered",
                             "o_squared", "y_ready"))
        st_out, ss_out = sem("state_p_out"), [sem(f"state_s_out{i}") for i in range(RH)]
        z_ready, z_out = sem("zeros_ready"), sem("zeros_out")
        outs_done = sem("latents_out")
        L = []
        for l in range(2):
            names = ("sc_zeroed logits_ready scores_ready mask_ready shT_ready route_ready tab_zero tab_zeroed scattered tab_in "
                     "th_done g_done gu_done ht_done y_done hb_ready sg_ready hid_ready hidT_ready yout_ready "
                     "idxc_ready idxc_seen comb_ready loop_end").split()
            d = {n: sem(f"{n}_{l}") for n in names}
            for n, k in (("rows_out", 2), ("w_in", 6), ("gathered", 2), ("stored", 2), ("got", 4)):
                d[n] = [sem(f"{n}{i}_{l}") for i in range(k)]
            L.append(d)
        msq_ready, ckv_ready, kpe_ready, cq_ready = (
            sem(n) for n in ("latent_squares_ready", "ckv_ready", "kpe_ready", "cq_ready"))
        ql_ready, qpe_ready, mx_ready, p_ready = (
            sem(n) for n in ("q_lat_ready", "q_pe_ready", "max_ready", "p_ready"))
        prodn_ready, smx_ready, se_ready, sp_ready, olr_ready = (
            sem(n) for n in ("new_products_ready", "s_max_ready", "s_exp_ready", "s_p_ready", "o_lat_ready"))
        orow_out = [sem(f"y_rows_out{i}") for i in range(2)]

        group_no, group_who, freed_by = {}, [], {"dve": 0, "act": 0}
        loads, load_no, landed, last_group, slot_count = [], {}, {}, {}, [0] * 6

        def pair(n):
            return PS[:, 2 * (n % 4):2 * (n % 4) + 2, :]

        def flat(g):
            return g.rearrange("p a b -> p (a b)")

        def xw(g):
            return g[:, :, 0:HALF]

        def smp(a):
            return a.rearrange("p (a b) -> p a b", a=2)

        def states(w):
            return w.rearrange("p (b t v) -> p b t v", b=NS, t=2)

        def state_rows(dram, h, t):
            return dram[0, :, h, t * P:(t + 1) * P, :].rearrange("b p v -> p b v")

        def h_tile(t, i):
            return hT[:, t, i // 2, (i % 2) * P:(i % 2) * P + P] if i < 4 else hS[:, t, :]

        block = ctx.enter_context(nc.Block())

        @block.tensor
        def _(pe):
            def claim(name, who):
                n = len(group_who)
                group_no[name] = n
                if n >= 4:
                    w, c = group_who[n - 4]
                    pe.wait_ge(took[w], c)
                freed_by[who] += 1
                group_who.append((who, freed_by[who]))
                return pair(n)

            def taken(name):
                w, c = group_who[group_no[name]]
                pe.wait_ge(took[w], c)

            def load(name, parts):
                k = len(loads)
                load_no[name] = k
                slot = k % 6
                loads.append((name, slot, parts))
                slot_count[slot] += 16 * (len(parts) if parts else 2 * NPAGE)
                landed[name] = slot_count[slot]
                pe.wait_ge(slot_in[slot], slot_count[slot])
                return W[:, slot, :]

            def used(name):
                last_group[load_no[name]] = len(group_who)

            def mm(out, lhsT, rhs, start=True, stop=True):
                return pe.matmul(out, lhsT=lhsT, rhs=rhs, start=start, stop=stop)

            def project(name, who, lhs, rhs, m=P):
                g = claim(name, who)
                for a in range(2):
                    for k in range(len(lhs)):
                        last = mm(g[0:m, a, 0:HALF], lhs[k], rhs[k][:, a, :], k == 0, k == len(lhs) - 1)
                last.then_inc(group_done, 1)

            def w3(w, t, n):
                return w[:, 0:t * n].rearrange("p (t n) -> p t n", t=t)

            ktile = lambda a: a.rearrange("(t p) n -> p t n", p=P)

            def ada_sum(u):
                src = A["w_ada"][u // 12][:, (u % 12) * 512:(u % 12) * 512 + 512] if u < 24 else \
                    A["kv_w_ada"][:, (u - 24) * 512:(u - 24) * 512 + 512]
                w = w3(load(("ada", u), [(lambda w: w3(w, DT, 512), ktile(src))]), DT, 512)
                g = flat(claim(("ada", u), "act"))
                for k in range(DT):
                    j = k % 4
                    last = mm(g[32 * j:32 * j + 32, 0:512], csT[:, k, :], w[:, k, :], k < 4, k >= 4)
                last.then_inc(group_done, 1)
                used(("ada", u))

            def ada_turn(u):
                taken(("ada", u))
                g = flat(claim(("at", u), "dve"))
                for c in range(4):
                    last = pe.transpose(g[:, c * P:(c + 1) * P], apart[:, u % 2, c * P:(c + 1) * P], ident)
                last.then_inc(group_done, 1)

            ada_next = [0]

            def fill(n=1):
                for _ in range(n):
                    u = ada_next[0]
                    ada_next[0] += 1
                    if u < ADA_UNITS:
                        ada_sum(u)
                    if 1 <= u <= ADA_UNITS:
                        ada_turn(u - 1)

            def norm_sum(k):
                pe.wait_ge(sq_ready, k + 1)
                project(("ss", k), "act", [ones] * DT, [hT[:, t, :, :] for t in range(DT)])

            def wait_h(k):
                pe.wait_ge(h_ready, k + 1)
                pe.wait_ge(hs_ready, k + 1)

            h_all = [hT[:, t, :, :] for t in range(DT)]

            pe.wait_ge(s_tab, 16)
            pe.wait_ge(s_rows, 16 * 9)
            pe.wait_ge(s_rb, 16)
            g = flat(claim("cols", "dve"))
            pe.transpose(g[:, 0:N_BIAS], brows[0:N_BIAS, :], ident[0:N_BIAS, 0:N_BIAS])
            pe.transpose(g[:, N_BIAS:N_BIAS + N_GAIN], grows[0:N_GAIN, :], ident[0:N_GAIN, 0:N_GAIN])
            mm(g[:, 512:512 + NE], ones[0:1, :], rbrow[0:1, :]).then_inc(group_done, 1)
            pe.wait_ge(csilu_ready, 1)
            g = flat(claim("cs", "act"))
            for t in range(DT):
                last = pe.transpose(g[:, t * NSEQ:(t + 1) * NSEQ], csilu[0:NSEQ, t * P:(t + 1) * P],
                                    ident[0:NSEQ, 0:NSEQ])
            last.then_inc(group_done, 1)
            taken("cs")
            pe.wait_ge(cs_zeroed, 1)
            fill(2)
            pe.wait_ge(s_x, 32)
            for i in range(5):
                g = flat(claim(("x", i), "dve"))
                n = P if i < 4 else NS
                for t in range(DT):
                    last = pe.transpose(g[:, t * P:t * P + n], xrows[0:n, i, t * P:(t + 1) * P], ident[0:n, 0:n])
                last.then_inc(group_done, 1)
            fill(3)

            norm_sum(0)
            wait_h(0)
            for h in range(RH):
                w_in = A["ret_w_in"][0]
                cut = lambda part: ktile(w_in[:, part * D + h * RD:part * D + (h + 1) * RD])
                halves = lambda a, b: [(lambda w: w3(w, DT, 512)[:, :, 0:RD], cut(a)),
                                       (lambda w: w3(w, DT, 512)[:, :, RD:512], cut(b))]
                w = w3(load(("qk", h), halves(0, 1)), DT, 512)
                for j, n in enumerate("qk"):
                    for t in range(2):
                        c = j * RD + t * P
                        project((n, h, t), "dve", [w[:, k, c:c + P] for k in range(DT)], h_all)
                used(("qk", h))
                w = w3(load(("vg", h), halves(2, 3)), DT, 512)
                g = flat(claim(("v", h), "act"))
                for i in range(4):
                    for k in range(DT):
                        last = mm(g[:, i * RD:(i + 1) * RD], h_tile(k, i), w[:, k, 0:RD],
                                  k == 0, k == DT - 1)
                last.then_inc(group_done, 1)
                g = flat(claim(("vs", h), "act"))
                for k in range(DT):
                    last = mm(g[0:NS, 0:RD], h_tile(k, 4), w[:, k, 0:RD], k == 0, k == DT - 1)
                last.then_inc(group_done, 1)
                for t in range(2):
                    c = RD + t * P
                    project(("g", h, t), "act", [w[:, k, c:c + P] for k in range(DT)], h_all)
                used(("vg", h))
                fill()
                pe.wait_ge(k_ready, h + 1)
                g = flat(claim(("kt", h), "act"))
                for j in range(4):
                    for t in range(2):
                        last = pe.transpose(g[:, j * RD + t * P:j * RD + (t + 1) * P], kT[:, t, j * P:(j + 1) * P],
                                            ident)
                last.then_inc(group_done, 1)
                g = flat(claim(("ks", h), "dve"))
                for t in range(2):
                    last = pe.transpose(g[0:NS, t * P:(t + 1) * P], kT[:, t, NP:T], ident)
                last.then_inc(group_done, 1)
                pe.wait_ge(q_ready, h + 1)
                for pr, js in (("sa", (0, 1)), ("sb", (2, 3))):
                    g = claim((pr, h), "dve")
                    for b, j in enumerate(js):
                        for t in range(2):
                            last = mm(g[:, b, 0:NP - P * j], kT[:, t, j * P:(j + 1) * P], qT[:, t, j * P:NP],
                                      t == 0, t == 1)
                    last.then_inc(group_done, 1)
                fill()
                taken(("sb", h))
                taken(("vs", h))
                g = claim(("o", h), "dve")
                for t in range(2):
                    for j in range(4):
                        last = mm(g[:, t, j * P:NP], vtok[:, j, t * P:(t + 1) * P], PT[j], j == 0, j == 3)
                last.then_inc(group_done, 1)
                taken(("kt", h))
                g = flat(claim(("st", h), "act"))
                for t in range(2):
                    for j in range(4):
                        last = mm(g[:, t * RD:(t + 1) * RD], kdec[:, j, t * P:(t + 1) * P], vtok[:, j, :],
                                  j == 0, j == 3)
                last.then_inc(group_done, 1)
                pe.wait_ge(km_ready, h + 1)
                for b2 in range(4):
                    g = claim(("kv", h, b2), "dve")
                    for b in range(2):
                        for t in range(2):
                            last = mm(g[:, b, t * RD:(t + 1) * RD], kmask[0:NS, 2 * b2 + b, t * P:(t + 1) * P],
                                      vtok[0:NS, 4, :])
                    last.then_inc(group_done, 1)
                fill()
                S = load(("S", h), [(lambda w, t=t: states(w)[:, :, t, :], state_rows(A["state_ret"], h, t))
                                    for t in range(2)])
                S = states(S)
                pe.wait_ge(st_updated, h + 1)
                g = claim(("os", h), "act")
                for a in range(2):
                    for d in range(2):
                        for j in range(4):
                            b = 4 * a + j
                            last = mm(g[32 * j:32 * j + 32, a, 0:RD],
                                      qT[:, d, NP + b:NP + b + 1].broadcast_to([P, 32]), S[:, b, d, :],
                                      d == 0, d == 1)
                last.then_inc(group_done, 1)
                used(("S", h))
                fill()
                taken(("os", h))
                g = flat(claim(("ot", h), "dve"))
                for t in range(2):
                    for a in range(2):
                        last = pe.transpose(g[:, (2 * t + a) * P:(2 * t + a + 1) * P],
                                            osb[:, a, t * P:(t + 1) * P], ident)
                last.then_inc(group_done, 1)
                pe.wait_ge(o_ready, h + 1)
                project(("mu", h), "dve", [inv256] * 2, [two(oT[:, t, :]) for t in range(2)])
                fill()
                pe.wait_ge(osq_ready, h + 1)
                project(("var", h), "act", [ones] * 2, [two(sq[:, t, :]) for t in range(2)])
                fill()
                w = load(("wout", h), [(lambda w: w3(w, 2, D), ktile(A["ret_w_out"][0][h * RD:(h + 1) * RD]))])
                w = w3(w, 2, D)
                pe.wait_ge(y_ready, h + 1)
                for t in range(DT):
                    project(("y", h, t), "dve", [w[:, k, t * P:(t + 1) * P] for k in range(2)],
                            [yT[:, k, :, :] for k in range(2)])
                used(("wout", h))
            fill(ADA_UNITS)

            def moe(l):
                s = L[l]
                nk = 1 + 3 * l
                norm_sum(nk)
                wait_h(nk)
                for i in range(5):
                    g = flat(claim(("ht", l, i), "act"))
                    n = P if i < 4 else NS
                    for t in range(DT):
                        last = pe.transpose(g[0:n, t * P:(t + 1) * P], h_tile(t, i), ident)
                    last.then_inc(group_done, 1)
                if l == 0:
                    pe.wait_ge(s_rw, 16)
                g = claim(("rt", l), "act")
                for k in range(DT):
                    j = k % 4
                    for a in range(2):
                        last = mm(g[32 * j:32 * j + 32, a, 0:HALF], rw[:, k, :], hT[:, k, a, :], k < 4, k >= 4)
                last.then_inc(group_done, 1)
                taken(("rt", l))
                g = flat(claim(("ru", l), "dve"))
                for i in range(5):
                    n = P if i < 4 else NS
                    src = lg[:, i // 2, (i % 2) * P:(i % 2) * P + P] if i < 4 else lgs
                    last = pe.transpose(g[0:n, i * P:(i + 1) * P], src, ident)
                last.then_inc(group_done, 1)
                w1 = w3(load(("wsg", l), [(lambda w: w3(w, DT, FE), ktile(A["shared_w_gate"][l]))]), DT, FE)
                w2 = w3(load(("wsu", l), [(lambda w: w3(w, DT, FE), ktile(A["shared_w_up"][l]))]), DT, FE)
                for f in range(FT):
                    project(("sg", l, f), "act", [w1[:, k, f * P:(f + 1) * P] for k in range(DT)], h_all)
                    project(("su", l, f), "dve", [w2[:, k, f * P:(f + 1) * P] for k in range(DT)], h_all)
                used(("wsg", l))
                used(("wsu", l))
                pe.wait_ge(s["mask_ready"], 1)
                g = flat(claim(("cnt", l), "dve"))
                M = R["M"].rearrange("p a b -> p (a b)")
                mm(g[:, 0:5 * NE], tri, M)
                mm(g[:, 512:512 + 5 * NE], ones, M).then_inc(group_done, 1)
                w = w3(load(("wsd", l), [(lambda w: w3(w, FT, D), ktile(A["shared_w_down"][l]))]), FT, D)
                pe.wait_ge(s["shT_ready"], FT)
                for t in range(DT):
                    project(("sd", l, t), "dve", [w[:, k, t * P:(t + 1) * P] for k in range(FT)],
                            [shT[:, k, :, :] for k in range(FT)])
                used(("wsd", l))
                pe.wait_ge(s["tab_in"], 16)
                g = flat(claim(("ix", l), "dve"))
                pe.transpose(g[:, 0:TABLE], tabr[0:TABLE, :], ident[0:TABLE, 0:TABLE]).then_inc(group_done, 1)

                base = len(loads) % 6
                s["base"] = base
                s["prior"] = len(loads)
                for w_, c_ in group_who[-4:]:
                    pe.wait_ge(took[w_], c_)
                psH = PS[:, 0:2, :].rearrange("p a b -> p (a b)")
                psG, psU = PS[:, 2, :], PS[:, 3, :]
                psX = PS[:, 4, :]
                psY = PS[:, 5:7, :]
                wg = [W[:, (base + 3 * u) % 6, :].rearrange("p (t n) -> p t n", t=DT) for u in range(2)]
                wu = [W[:, (base + 3 * u + 1) % 6, :].rearrange("p (t n) -> p t n", t=DT) for u in range(2)]
                wd = [W[:, (base + 3 * u + 2) % 6, :].rearrange("p (t n) -> p t n", t=FT) for u in range(2)]

                def turn_h(u):
                    for t in range(DT):
                        last = pe.transpose(psH[:, t * P:(t + 1) * P], hblk[u][:, t * P:(t + 1) * P], ident)
                    last.then_inc(s["th_done"], 1)

                def block_of(it, u, first):
                    b = it * 2 + u
                    land = it * 16 + 16
                    pe.wait_ge(s["w_in"][3 * u], land)
                    pe.wait_ge(s["hb_ready"], b + 1)
                    if not first:
                        pe.wait_ge(s["sg_ready"], b)
                    for k in range(DT):
                        last = mm(psG, hbT[u][:, k, :], wg[u][:, k, :], k == 0, k == DT - 1)
                    last.then_inc(s["g_done"], 1)
                    pe.wait_ge(s["w_in"][3 * u + 1], land)
                    if not first:
                        pe.wait_ge(s["hid_ready"], b)
                    for k in range(DT):
                        last = mm(psU, hbT[u][:, k, :], wu[u][:, k, :], k == 0, k == DT - 1)
                    last.then_inc(s["gu_done"], 1)
                    pe.wait_ge(s["gathered"][1 - u], (it + u) * 16 + 16)
                    turn_h(1 - u)
                    pe.wait_ge(s["hid_ready"], b + 1)
                    if not first:
                        pe.wait_ge(s["hidT_ready"], b)
                    for f in range(FT):
                        last = pe.transpose(psX[:, f * P:(f + 1) * P], hid[:, f * P:(f + 1) * P], ident)
                    last.then_inc(s["ht_done"], 1)
                    pe.wait_ge(s["w_in"][3 * u + 2], land)
                    pe.wait_ge(s["hidT_ready"], b + 1)
                    if not first:
                        pe.wait_ge(s["yout_ready"], b)
                    for n in range(2):
                        for f in range(FT):
                            last = mm(psY[:, n, :], hidT[:, f, :], wd[u][:, f, n * 512:(n + 1) * 512],
                                      f == 0, f == FT - 1)
                    last.then_inc(s["y_done"], 1)

                pe.wait_ge(s["gathered"][0], 16)
                turn_h(0)
                block_of(0, 0, True)
                block_of(0, 1, False)
                pe.wait_ge(s["route_ready"], 1)
                n_it = pe.value_load(niter[0:1, 0:1], min_val=8, max_val=MAXBLK // 2)
                with pe.Fori(1, n_it) as it:
                    for u in range(2):
                        block_of(it, u, False)
                pe.wait_ge(s["loop_end"], 1)
                for i in range(5):
                    pe.wait_ge(s["comb_ready"], i + 1)
                    g = flat(claim(("cb", l, i), "dve"))
                    n = P if i < 4 else NS
                    for t in range(DT):
                        last = pe.transpose(g[:, t * P:t * P + n],
                                            hbT[i % 2].rearrange("p t n -> p (t n)")[0:n, t * P:(t + 1) * P],
                                            ident[0:n, 0:n])
                    last.then_inc(group_done, 1)

            moe(0)

            norm_sum(2)
            wait_h(2)
            w = w3(load("dkv", [(lambda w: w3(w, DT, LAT + ROPE), ktile(A["mla_w_dkv"]))]), DT, LAT + ROPE)
            for t in range(2):
                project(("z", t), "act", [w[:, k, t * P:(t + 1) * P] for k in range(DT)], h_all)
            project("zk", "act", [w[:, k, LAT:LAT + ROPE] for k in range(DT)], h_all, ROPE)
            used("dkv")
            taken("zk")
            project("kr", "dve", [cst("rot")[0:ROPE, :]], [zk[0:ROPE, :, :]], ROPE)
            pe.wait_ge(msq_ready, 1)
            project("zss", "act", [ones] * 2, [msq[:, t, :, :] for t in range(2)])
            pe.wait_ge(ckv_ready, 1)
            pe.wait_ge(kpe_ready, 1)
            for i0 in (0, 2, 4):
                g = claim(("ct", i0), "act")
                for i in range(i0, min(i0 + 2, 5)):
                    n = P if i < 4 else NS
                    for t in range(2):
                        pe.transpose(g[0:n, i - i0, t * P:(t + 1) * P], ckvT[:, t, i * P:i * P + n], ident)
                    last = pe.transpose(g[0:n, i - i0, LAT:LAT + ROPE], kpeT[0:ROPE, i * P:i * P + n],
                                        ident[0:ROPE, 0:ROPE])
                last.then_inc(group_done, 1)

            norm_sum(3)
            wait_h(3)
            w = w3(load("dq", [(lambda w: w3(w, DT, LAT), ktile(A["mla_w_dq"][0]))]), DT, LAT)
            for t in range(2):
                project(("cq", t), "act", [w[:, k, t * P:(t + 1) * P] for k in range(DT)], h_all)
            used("dq")
            w = w3(load("uv", [(lambda w: w3(w, MH, LAT), A["mla_w_uv"].rearrange("h v c -> v h c"))]), MH, LAT)
            for half in range(2):
                g = flat(claim(("uv", half), "act"))
                for j in range(8):
                    h, t = half * 4 + j // 2, j % 2
                    last = pe.transpose(g[:, j * P:(j + 1) * P], w[:, h, t * P:(t + 1) * P], ident)
                last.then_inc(group_done, 1)
            used("uv")
            pe.wait_ge(msq_ready, 2)
            project("qss", "act", [ones] * 2, [msq[:, t, :, :] for t in range(2)])
            pe.wait_ge(cq_ready, 1)
            QW = NOPE + ROPE
            wq = w3(load("uq", [(lambda w: w3(w, 2, MH * QW), ktile(A["mla_w_uq"][0]))]), 2, MH * QW)
            wk = w3(load("uk", [(lambda w: w3(w, MH, LAT), A["mla_w_uk"].rearrange("h n c -> n h c"))]), MH, LAT)
            cq_all = [cqT[:, k, :, :] for k in range(2)]
            def query(h):
                project(("qn", h), "act", [wq[:, k, h * QW:h * QW + NOPE] for k in range(2)], cq_all)
                project(("qp", h), "act", [wq[:, k, h * QW + NOPE:(h + 1) * QW] for k in range(2)], cq_all, ROPE)
                taken(("qn", h))
                for t in range(2):
                    project(("ql", h, t), "dve", [wk[:, h, t * P:(t + 1) * P]], [qn])
                taken(("qp", h))
                project(("qr", h), "dve", [cst("rot")[0:ROPE, :]], [qpr[0:ROPE, :, :]], ROPE)

            query(0)
            for h in range(MH):
                pe.wait_ge(ql_ready, h + 1)
                pe.wait_ge(qpe_ready, h + 1)
                for name, chunks in SCORES:
                    g = flat(claim((name, h), "act"))
                    for i, at in chunks:
                        o = g[:, at:at + (i + 1) * P]
                        for t in range(2):
                            mm(o, ql[:, t, i * P:(i + 1) * P], ckvT[:, t, 0:(i + 1) * P], t == 0, False)
                        last = mm(o, qpe[0:ROPE, i * P:(i + 1) * P], kpeT[0:ROPE, 0:(i + 1) * P], False, True)
                    last.then_inc(group_done, 1)
                if h + 1 < MH:
                    query(h + 1)
                pe.wait_ge(p_ready, h + 1)
                for name, chunks in TURNS:
                    g = flat(claim((name, h), "act"))
                    for i, at in chunks:
                        for j in range(i + 1):
                            last = pe.transpose(g[:, at + j * P:at + (j + 1) * P], pr_[:, TRI[i] + j * P:TRI[i] + (j + 1) * P],
                                                ident)
                    last.then_inc(group_done, 1)
                taken(("ptb", h))
                g = claim(("ol", h), "dve")
                for t in range(2):
                    for j in range(4):
                        last = mm(g[:, t, j * P:NP], ctok[:, j, t * P:(t + 1) * P], PTm[:, j, j * P:NP],
                                  j == 0, j == 3)
                last.then_inc(group_done, 1)
                taken(("ol", h))
                g = claim(("ov", h), "act")
                for t in range(2):
                    last = mm(g[:, 0, :], uvT[:, h, t, :], olat[:, t, :], t == 0, t == 1)
                last.then_inc(group_done, 1)
            used("uq")
            used("uk")
            for q in range(2):
                pages = {}
                for j in range(4):
                    b = 4 * q + j
                    pages[b] = w3(load(("pages", b), None), NPAGE, LAT + ROPE)
                    for t in range(3):
                        g = flat(claim(("kt3", b, t), "act" if t % 2 else "dve"))
                        m = P if t < 2 else ROPE
                        for pg in range(NPAGE):
                            last = pe.transpose(g[0:m, pg * P:(pg + 1) * P], pages[b][:, pg, t * P:t * P + m], ident)
                        last.then_inc(group_done, 1)
                    for t in range(3):
                        taken(("kt3", b, t))
                    g = flat(claim(("sp", b), "dve"))
                    for t in range(3):
                        m = P if t < 2 else ROPE
                        for c in range(4):
                            last = mm(g[32 * c:32 * c + 32, 0:256], qsl[0:m, t, b, :],
                                      KT[0:m, t, c * 256:(c + 1) * 256], t == 0, t == 2)
                    last.then_inc(group_done, 1)
                pe.wait_ge(prodn_ready, q + 1)
                g = flat(claim(("sn", q), "dve"))
                for t in range(3):
                    m = P if t < 2 else ROPE
                    last = mm(g[:, 0:1], prodn[0:m, t, :], ones[0:m, 0:1], t == 0, t == 2)
                last.then_inc(group_done, 1)
                pe.wait_ge(sp_ready, q + 1)
                g = flat(claim(("pts", q), "act"))
                for pg in range(NPAGE):
                    last = pe.transpose(g[:, pg * P:(pg + 1) * P], Ps[:, pg * P:(pg + 1) * P], ident)
                last.then_inc(group_done, 1)
                taken(("pts", q))
                g = claim(("pv", q), "dve")
                mm(g[:, 1, 0:LAT], cst("selq")[0:NS, q * P:(q + 1) * P], ctok[0:NS, 4, 0:LAT])
                for pg in range(NPAGE):
                    for j in range(4):
                        last = mm(g[32 * j:32 * j + 32, 0, 0:LAT], PTs[:, pg, 32 * j:32 * j + 32],
                                  pages[4 * q + j][:, pg, 0:LAT], pg == 0, pg == NPAGE - 1)
                last.then_inc(group_done, 1)
                pe.wait_ge(olr_ready, q + 1)
                g = flat(claim(("olt", q), "dve"))
                for t in range(2):
                    last = pe.transpose(g[:, t * P:(t + 1) * P], olr[:, t * P:(t + 1) * P], ident)
                last.then_inc(group_done, 1)
                for j in range(4):
                    used(("pages", 4 * q + j))
            taken(("olt", 1))
            g = flat(claim("ovs", "act"))
            for h in range(MH):
                for t in range(2):
                    last = mm(g[:, h * NS:(h + 1) * NS], uvT[:, h, t, :], osl[:, t, :, h], t == 0, t == 1)
            last.then_inc(group_done, 1)
            taken(("ov", MH - 1))
            taken("ovs")
            for c in range(2):
                w = w3(load(("wo", c), [(lambda w: w3(w, DT, 512), ktile(A["mla_w_o"][0][:, c * 512:(c + 1) * 512]))]),
                       DT, 512)
                for t in range(4):
                    project(("mo", 4 * c + t), "dve", [w[:, k, t * P:(t + 1) * P] for k in range(DT)], h_all)
                used(("wo", c))

            moe(1)

            norm_sum(5)
            pe.wait_ge(hs_ready, 6)
            for i in range(5):
                g = flat(claim(("out", i), "act"))
                n = P if i < 4 else NS
                for t in range(DT):
                    last = pe.transpose(g[0:n, t * P:(t + 1) * P], h_tile(t, i), ident)
                last.then_inc(group_done, 1)

        seen = {"dve": 0, "act": 0}

        def group(eng, who, name):
            n = group_no[name]
            seen[who] += 1
            assert group_who[n] == (who, seen[who]), (name, group_who[n], seen[who])
            eng.wait_ge(group_done, n + 1)
            return pair(n)

        @block.scalar
        def _(act):
            chain = [0]
            act_chain = sem("act_chain")

            def link(ins):
                chain[0] += 1
                ins.then_inc(act_chain, 1)
                act.wait_ge(act_chain, chain[0])

            def grp(name):
                return group(act, "act", name)

            freed = took["act"]
            cp = lambda o, i, **k: act.activation(o, i, ACT.Copy, **k)

            act.dma_start(C[:, :], A["tables"]).then_inc(s_tab, 16)
            act.dma_start(crow[0:1, :], A["c_prompt"]).then_inc(s_c, 16)
            act.dma_start(crow[1:NSEQ, :], A["c_sample"]).then_inc(s_c, 16)
            rows = lambda a: a.rearrange("(t p) -> t p", p=P)
            act.dma_start(brows[0:96, :], A["b_ada"].rearrange("l (t p) -> (l t) p", p=P)).then_inc(s_rows, 16)
            act.dma_start(brows[96:112, :], rows(A["kv_b_ada"])).then_inc(s_rows, 16)
            act.dma_start(grows[G_MIX:G_FFN, :], A["norm_mix_g"].rearrange("l (t p) -> (l t) p", p=P)).then_inc(s_rows, 16)
            act.dma_start(grows[G_FFN:G_KV, :], A["norm_ffn_g"].rearrange("l (t p) -> (l t) p", p=P)).then_inc(s_rows, 16)
            act.dma_start(grows[G_KV:G_GN, :], rows(A["kv_norm_g"])).then_inc(s_rows, 16)
            act.dma_start(grows[G_GN:G_FIN, :], A["ret_gn_g"].rearrange("l (t p) -> (l t) p", p=P)).then_inc(s_rows, 16)
            act.dma_start(grows[G_FIN:G_CKV, :], rows(A["final_norm_g"])).then_inc(s_rows, 16)
            act.dma_start(grows[G_CKV:G_CQ, :], rows(A["mla_kv_norm_g"])).then_inc(s_rows, 16)
            act.dma_start(grows[G_CQ:N_GAIN, :], A["mla_q_norm_g"].rearrange("l (t p) -> (l t) p", p=P)).then_inc(s_rows, 16)
            act.wait_ge(s_c, 32)
            act.activation(csilu[0:NSEQ, :], crow[0:NSEQ, :], ACT.Silu).then_inc(csilu_ready, 1)
            g = flat(grp("cs"))
            act.wait_ge(cs_zeroed, 1)
            cp(csT[:, :, 0:NSEQ], g[:, 0:DT * NSEQ].rearrange("p (a b) -> p a b", a=DT)).then_inc(freed, 1)
            ada_next = [0]

            def fill(n=1):
                for _ in range(n):
                    u = ada_next[0]
                    ada_next[0] += 1
                    if u < ADA_UNITS:
                        g = flat(grp(("ada", u)))
                        cp(apart[:, u % 2, 0:512], g[:, 0:512]).then_inc(freed, 1)

            fill(5)

            def norm(k, x_need, shift):
                act.wait_ge(x_updated, x_need)
                for t in range(DT):
                    last = act.activation(hT[:, t, :, :], xT[:, t, :, :], ACT.Square, scale=D ** -0.5)
                last.then_inc(sq_ready, 1)
                g = grp(("ss", k))
                act.activation(rs[:, :, :], xw(g), ACT.Sqrt, bias=cst("eps")).then_inc(freed, 1)
                if shift is not None:
                    for t in range(DT):
                        act.wait_ge(h_scaled, 8 * k + t + 1)
                        last = act.activation(hT[:, t, :, 0:HP], hT[:, t, :, 0:HP], ACT.Identity,
                                              bias=mod[:, shift + t, 0:1])
                    last.then_inc(h_ready, 1)

            norm(0, 5, 0)
            for h in range(RH):
                g = flat(grp(("v", h)))
                cp(vtok[:, 0:4, :].rearrange("p a b -> p (a b)"), g).then_inc(freed, 1)
                g = flat(grp(("vs", h)))
                act.activation(vtok[0:NS, 4, :], g[0:NS, 0:RD], ACT.Copy).then_inc(freed, 1)
                for t in range(2):
                    g = grp(("g", h, t))
                    act.activation(gT[:, t, :, :], xw(g), ACT.Silu).then_inc(freed, 1)
                fill()
                g = flat(grp(("kt", h)))
                for j in range(4):
                    s0 = AT["kdec"][0] + 4 * h + j
                    last = cp(kdec[:, j, :], g[:, j * RD:(j + 1) * RD], scale=C[:, s0:s0 + 1])
                last.then_inc(freed, 1)
                fill()
                g = flat(grp(("st", h)))
                if h:
                    act.wait_ge(st_out, 16 * h)
                else:
                    act.wait_ge(z_out, 16 * 2 * (MAXBLK - NE))
                cp(stout.rearrange("p a b -> p (a b)"), g[:, 0:2 * RD]).then_inc(freed, 1)
                act.wait_ge(freed, seen["act"])
                act.dma_start(O["state_p"][0, 0, h].rearrange("(t p) v -> p t v", p=P), stout).then_inc(st_out, 16)
                act.wait_ge(st_updated, h + 1)
                slot = load_no[("S", h)] % 6
                for t in range(2):
                    act.dma_start(state_rows(O["state_s"], h, t),
                                  states(W[:, slot, :])[:, :, t, :]).then_inc(ss_out[h], 16)
                fill()
                g = grp(("os", h))
                cp(osb, g[:, :, 0:RD]).then_inc(freed, 1)
                fill()
                act.wait_ge(oc_ready, h + 1)
                act.activation(sq.rearrange("p a b -> p (a b)"), oT.rearrange("p a b -> p (a b)"), ACT.Square,
                               scale=RD ** -0.5).then_inc(osq_ready, 1)
                fill()
                g = grp(("var", h))
                act.activation(rs2, xw(g), ACT.Sqrt, bias=cst("eps")).then_inc(freed, 1)
                fill()
            fill(ADA_UNITS)

            def moe(l, x_need):
                s = L[l]
                norm(1 + 3 * l, x_need, 48 * l + 24)
                for i in range(5):
                    g = flat(grp(("ht", l, i)))
                    n = P if i < 4 else NS
                    if i >= 2:
                        act.wait_ge(s["rows_out"][i % 2], 16 * (i // 2))
                    cp(ysb[i % 2][0:n, :], g[0:n, :]).then_inc(freed, 1)
                    act.wait_ge(freed, seen["act"])
                    act.dma_start(h_dram[l][i * P:i * P + n, :], ysb[i % 2][0:n, :]).then_inc(s["rows_out"][i % 2], 16)
                g = grp(("rt", l))
                cp(lgs.rearrange("p (a b) -> p a b", a=2), g[:, :, HP:HALF])
                cp(lg, xw(g)).then_inc(freed, 1)
                act.wait_ge(s["logits_ready"], 1)
                act.activation(R["sc"][:, 0:4, :], R["sc"][:, 0:4, :], ACT.Sigmoid)
                act.activation(R["sc"][0:NS, 4, :], R["sc"][0:NS, 4, :], ACT.Sigmoid).then_inc(s["scores_ready"], 1)
                for f in range(FT):
                    g = grp(("sg", l, f))
                    if f:
                        act.wait_ge(s["shT_ready"], f)
                    act.activation(sgs, xw(g), ACT.Silu).then_inc(freed, 1)
                psH = PS[:, 0:2, :].rearrange("p a b -> p (a b)")

                def turn(u, need):
                    act.wait_ge(s["th_done"], need)
                    cp(hbT[u].rearrange("p t n -> p (t n)"), psH).then_inc(s["hb_ready"], 1)

                def block_of(it, u):
                    b = it * 2 + u
                    act.wait_ge(s["g_done"], b + 1)
                    act.activation(sg, PS[:, 2, :], ACT.Silu).then_inc(s["sg_ready"], 1)
                    turn(1 - u, b + 2)

                turn(0, 1)
                block_of(0, 0)
                act.wait_ge(s["hid_ready"], 1)
                block_of(0, 1)
                act.wait_ge(s["route_ready"], 1)
                n_it = act.value_load(niter[0:1, 0:1], min_val=8, max_val=MAXBLK // 2)
                with act.Fori(1, n_it) as it:
                    for u in range(2):
                        act.wait_ge(s["hid_ready"], it * 2 + u)
                        block_of(it, u)

            moe(0, 5 + DT * RH)
            XN = 5 + DT * RH + DT + 5
            norm(2, XN, 96)
            for t in range(2):
                g = grp(("z", t))
                cp(zT[:, t, :, :], xw(g)).then_inc(freed, 1)
            g = grp("zk")
            cp(zk[0:ROPE, :, :], xw(g)[0:ROPE]).then_inc(freed, 1)
            act.wait_ge(freed, seen["act"])
            for t in range(2):
                last = act.activation(msq[:, t, :, :], zT[:, t, :, :], ACT.Square, scale=LAT ** -0.5)
            last.then_inc(msq_ready, 1)
            g = grp("zss")
            act.activation(rs[:, :, :], xw(g), ACT.Sqrt, bias=cst("eps")).then_inc(freed, 1)
            for i0 in (0, 2, 4):
                g = grp(("ct", i0))
                if i0 < 4:
                    cp(ctok[:, i0:i0 + 2, :], g[:, :, 0:LAT + ROPE]).then_inc(freed, 1)
                else:
                    cp(ctok[0:NS, 4, :], g[0:NS, 0, 0:LAT + ROPE]).then_inc(freed, 1)
            act.wait_ge(freed, seen["act"])
            act.dma_start(O["ckv_p"][0].rearrange("(i p) c -> p i c", p=P), ctok[:, 0:4, 0:LAT]).then_inc(outs_done, 16)
            act.dma_start(O["kpe_p"][0].rearrange("(i p) c -> p i c", p=P), ctok[:, 0:4, LAT:]).then_inc(outs_done, 16)
            act.dma_start(O["ckv_s"].rearrange("b a c -> (b a) c"), ctok[0:NS, 4, 0:LAT]).then_inc(outs_done, 16)
            act.dma_start(O["kpe_s"].rearrange("b a c -> (b a) c"), ctok[0:NS, 4, LAT:]).then_inc(outs_done, 16)
            act.wait_ge(ckv_ready, 1)
            norm(3, XN, 48)
            for t in range(2):
                g = grp(("cq", t))
                cp(zT[:, t, :, :], xw(g)).then_inc(freed, 1)
            act.wait_ge(freed, seen["act"])
            for t in range(2):
                last = act.activation(msq[:, t, :, :], zT[:, t, :, :], ACT.Square, scale=LAT ** -0.5)
            last.then_inc(msq_ready, 1)
            for half in range(2):
                g = flat(grp(("uv", half)))
                cp(uvT[:, 4 * half:4 * half + 4, :, :].rearrange("p a b c -> p (a b c)"), g).then_inc(freed, 1)
            g = grp("qss")
            act.activation(rs[:, :, :], xw(g), ACT.Sqrt, bias=cst("eps")).then_inc(freed, 1)
            def query(h):
                g = grp(("qn", h))
                cp(qn, xw(g)).then_inc(freed, 1)
                g = grp(("qp", h))
                if h:
                    act.wait_ge(qpe_ready, h)
                cp(qpr[0:ROPE, :, :], xw(g)[0:ROPE]).then_inc(freed, 1)

            query(0)
            for h in range(MH):
                act.wait_ge(mx_ready, h + 1)
                for name, chunks in SCORES:
                    g = flat(grp((name, h)))
                    for i, at in chunks:
                        last = act.activation(pr_[:, TRI[i]:TRI[i + 1]], g[:, at:at + (i + 1) * P], ACT.Exp,
                                              scale=MLA_SCALE, bias=mcol[:, 4 + i:5 + i],
                                              accum_out=mcol[:, 8 + i:9 + i])
                    last.then_inc(freed, 1)
                if h + 1 < MH:
                    query(h + 1)
                for name, chunks in TURNS:
                    g = flat(grp((name, h)))
                    for i, at in chunks:
                        last = cp(PTm[:, 0:i + 1, i * P:(i + 1) * P],
                                  g[:, at:at + (i + 1) * P].rearrange("p (a b) -> p a b", a=i + 1))
                    last.then_inc(freed, 1)
                g = grp(("ov", h))
                cp(hT[:, h, :, 0:HP], g[:, 0, :].rearrange("p (a b) -> p a b", a=2)).then_inc(freed, 1)
            for q in range(2):
                for j in range(4):
                    b = 4 * q + j
                    g = flat(grp(("kt3", b, 1)))
                    cp(KT[:, 1, :], g).then_inc(freed, 1)
                act.wait_ge(smx_ready, q + 1)
                act.activation(Ps, S_sb, ACT.Exp, scale=MLA_SCALE, bias=mcol2[:, 1:2],
                               accum_out=mcol2[:, 2:3]).then_inc(se_ready, 1)
                g = flat(grp(("pts", q)))
                cp(PTs.rearrange("p a b -> p (a b)"), g).then_inc(freed, 1)
            g = flat(grp("ovs"))
            cp(hT[:, :, :, HP:HALF], g[:, 0:MH * NS].rearrange("p (h a b) -> p h a b", h=MH, a=2)).then_inc(freed, 1)
            act.wait_ge(outs_done, 64)
            moe(1, XN + DT)
            norm(5, XN + DT + DT + 5, None)
            for i in range(5):
                g = flat(grp(("out", i)))
                n = P if i < 4 else NS
                if i >= 2:
                    act.wait_ge(orow_out[i % 2], 16 * (i // 2))
                cp(orow[i % 2][0:n, :], g[0:n, :]).then_inc(freed, 1)
                act.wait_ge(freed, seen["act"])
                dst = O["y_p"][0][i * P:(i + 1) * P, :] if i < 4 else O["y_s"].rearrange("b a c -> (b a) c")
                act.dma_start(dst, orow[i % 2][0:n, :]).then_inc(orow_out[i % 2], 16)
            act.wait_ge(orow_out[0], 48)
            act.wait_ge(orow_out[1], 32)
            act.wait_ge(st_out, 16 * RH)
            for h in range(RH):
                act.wait_ge(ss_out[h], 32)

        @block.vector
        def _(dve):
            chain = [0]

            def link(ins):
                chain[0] += 1
                ins.then_inc(dve_chain, 1)
                dve.wait_ge(dve_chain, chain[0])

            def settled(own):
                dve.wait_ge(took["dve"], seen["dve"])

            def grp(name):
                return group(dve, "dve", name)

            def act_took(name):
                w, c = group_who[group_no[name]]
                assert w == "act"
                dve.wait_ge(took[w], c)

            freed = took["dve"]
            tt, ts, stt = dve.tensor_tensor, dve.tensor_scalar, dve.scalar_tensor_tensor
            wide = lambda a, shape: a.broadcast_to(shape)

            ada_next = [0]

            def fill(n=1):
                for _ in range(n):
                    u = ada_next[0] - 1
                    ada_next[0] += 1
                    if 0 <= u < ADA_UNITS:
                        g = flat(grp(("at", u)))
                        part = g[:, 0:512].rearrange("p (c j r) -> p c r j", c=4, j=4)[:, :, 0:NSEQ, :]
                        out = asum[:, u % 2, :].rearrange("p (a b) -> p a b", a=4)
                        if u >= 2:
                            dve.wait_ge(ada_ready, u - 1)
                        dve.tensor_reduce(out, part, AX.X, ALU.add).then_inc(freed, 1)
                        settled("asum")
                        tt(mod[:, 4 * u:4 * u + 4, :], out,
                           wide(cols[:, 4 * u:4 * u + 4].unsqueeze(2), [P, 4, NSEQ]), ALU.add).then_inc(ada_ready, 1)

            def mods_ready(j):
                dve.wait_ge(ada_ready, j // 4 + 1)

            def norm(k, shift, gain, modulated=True):
                g8 = cols[:, N_BIAS + gain:N_BIAS + gain + DT]
                if modulated:
                    mods_ready(shift + 15)
                    link(stt(acol[:, :, :], mod[:, shift + 8:shift + 16, :], 1.0,
                             wide(g8.unsqueeze(2), [P, DT, NSEQ]), ALU.add, ALU.mult))
                act_took(("ss", k))
                link(dve.reciprocal(rs[:, :, :], rs[:, :, :]))
                for t in range(DT):
                    scale = acol[:, t, 0:1] if modulated else g8[:, t:t + 1]
                    stt(hT[:, t, :, 0:HP], xT[:, t, :, 0:HP], scale, rs[:, :, 0:HP],
                        ALU.mult, ALU.mult).then_inc(h_scaled, 1)
                hs, xs = hT[:, :, :, HP:HALF], xT[:, :, :, HP:HALF]
                link(tt(hs, xs, wide(rs[:, :, HP:HALF].unsqueeze(1), [P, DT, 2, HS]), ALU.mult))
                if modulated:
                    link(tt(hs, hs, acol[:, :, 1:NSEQ].rearrange("p t (a b) -> p t a b", a=2), ALU.mult))
                    link(tt(hs, hs, mod[:, shift:shift + DT, 1:NSEQ].rearrange("p t (a b) -> p t a b", a=2),
                            ALU.add))
                else:
                    link(tt(hs, hs, wide(g8.unsqueeze(2), [P, DT, NS]).rearrange("p t (a b) -> p t a b", a=2),
                            ALU.mult))
                dve.tensor_copy(hS[:, :, :].rearrange("p t (a b) -> p t a b", a=2), hs).then_inc(hs_ready, 1)

            xup = [5]

            def residual(name, t, gate):
                g = grp(name)
                if t == 0:
                    mods_ready(gate + 7)
                    dve.wait_ge(x_updated, xup[0])
                link(tt(tmp8[:, t, :, :], xw(g)[:, :, HP:HALF], smp(mod[:, gate + t, 1:NSEQ]), ALU.mult))
                stt(xT[:, t, :, 0:HP], g[:, :, 0:HP], mod[:, gate + t, 0:1], xT[:, t, :, 0:HP],
                    ALU.mult, ALU.add).then_inc(freed, 1)
                tt(xT[:, t, :, HP:HALF], xT[:, t, :, HP:HALF], tmp8[:, t, :, :], ALU.add).then_inc(x_updated, 1)
                xup[0] += 1

            dve.memset(ztile, 0.0).then_inc(z_ready, 1)
            dve.memset(csT[:, :, :], 0.0).then_inc(cs_zeroed, 1)
            dve.memset(rw[:, :, :], 0.0).then_inc(rw_zeroed, 1)
            g = flat(grp("cols"))
            dve.tensor_copy(cols[:, :], g[:, 0:N_BIAS + N_GAIN])
            dve.tensor_copy(rbias[:, :], g[:, 512:512 + NE]).then_inc(freed, 1)
            settled("cols")
            fill(2)
            for i in range(5):
                g = flat(grp(("x", i)))
                n = P if i < 4 else NS
                src = g.rearrange("p (t n) -> p t n", t=DT)[:, :, 0:n]
                if i < 4:
                    dve.tensor_copy(xT[:, :, i // 2, (i % 2) * P:(i % 2) * P + P], src).then_inc(freed, 1)
                else:
                    dve.tensor_copy(xT[:, :, :, HP:HALF], src.rearrange("p t (a b) -> p t a b", a=2)).then_inc(freed, 1)
                dve.wait_ge(freed, seen["dve"])
                dve.sem_inc(x_updated, 1)
            fill(3)

            norm(0, 0, G_MIX)

            def rotate(n, h, out, ready):
                if n == "k":
                    dve.wait_ge(q_ready, h + 1)
                elif h:
                    dve.wait_ge(k_ready, h)
                g0 = grp((n, h, 0))
                tt(rt[0], xw(g0), cosr, ALU.mult)
                tt(rt[2], xw(g0), sinr, ALU.mult).then_inc(freed, 1)
                g1 = grp((n, h, 1))
                tt(rt[1], xw(g1), sinr, ALU.mult)
                tt(rt[3], xw(g1), cosr, ALU.mult).then_inc(freed, 1)
                settled("rt")
                for t, (a, b, op) in enumerate(((0, 1, ALU.subtract), (2, 3, ALU.add))):
                    tt(two(out[:, t, 0:NP]), rt[a][:, :, 0:HP], rt[b][:, :, 0:HP], op)
                    last = tt(two(out[:, t, NP:T]), rt[a][:, :, HP:HALF], rt[b][:, :, HP:HALF], op)
                last.then_inc(ready, 1)

            for h in range(RH):
                rotate("q", h, qT, q_ready)
                rotate("k", h, kT, k_ready)
                fill()
                g = flat(grp(("ks", h)))
                dve.tensor_copy(ks[0:NS, :], g[0:NS, 0:RD]).then_inc(freed, 1)
                settled("ks")
                dve.wait_ge(k_ready, h + 1)
                tt(kmask[0:NS, :, :], wide(ks[0:NS, :].unsqueeze(1), [NS, NS, RD]),
                   wide(ident[0:NS, 0:NS].unsqueeze(2), [NS, NS, RD]), ALU.mult).then_inc(km_ready, 1)
                for pr, js in (("sa", (0, 1)), ("sb", (2, 3))):
                    g = grp((pr, h))
                    for b, j in enumerate(js):
                        last = tt(PT[j], g[:, b, 0:NP - P * j], decay[:, h, 0:NP - P * j], ALU.mult)
                    last.then_inc(freed, 1)
                fill()
                g = grp(("o", h))
                dve.tensor_copy(oT[:, :, 0:NP], g).then_inc(freed, 1)
                name = ("S", h)
                slot = load_no[name] % 6
                S = W[:, slot, :].rearrange("p (b n) -> p b n", b=NS)
                dve.wait_ge(slot_in[slot], landed[name])
                for b2 in range(4):
                    g = grp(("kv", h, b2))
                    for b in range(2):
                        last = stt(S[:, 2 * b2 + b, :], S[:, 2 * b2 + b, :], float(np.float32(1 - 2.0 ** (-5 - h))),
                                   g[:, b, :], ALU.mult, ALU.add)
                    last.then_inc(freed, 1)
                settled("S")
                dve.sem_inc(st_updated, 1)
                fill()
                fill()
                g = flat(grp(("ot", h)))
                ts(oT[:, :, NP:T], g[:, 0:512].rearrange("p (t b r) -> p t b r", t=2, r=32)[:, :, :, 0], RD ** -0.5,
                   None, ALU.mult).then_inc(freed, 1)
                settled("o")
                dve.sem_inc(o_ready, 1)
                g = grp(("mu", h))
                for t in range(2):
                    last = tt(two(oT[:, t, :]), two(oT[:, t, :]), xw(g), ALU.subtract)
                last.then_inc(freed, 1)
                settled("oc")
                dve.sem_inc(oc_ready, 1)
                fill(2)
                act_took(("var", h))
                link(dve.reciprocal(rs2, rs2))
                r = rs2.rearrange("p a b -> p (a b)")
                for t in range(2):
                    last = tt(oT[:, t, :], oT[:, t, :], r, ALU.mult)
                link(last)
                act_took(("g", h, 1))
                for t in range(2):
                    gn = cols[:, N_BIAS + G_GN + 2 * h + t:N_BIAS + G_GN + 2 * h + t + 1]
                    stt(yT[:, t, :, 0:HP], two(oT[:, t, 0:NP]), gn, gT[:, t, :, 0:HP], ALU.mult, ALU.mult)
                    last = stt(yT[:, t, :, HP:HALF], two(oT[:, t, NP:T]), gn, gT[:, t, :, HP:HALF],
                               ALU.mult, ALU.mult)
                last.then_inc(y_ready, 1)
                for t in range(DT):
                    residual(("y", h, t), t, 16)
            fill(ADA_UNITS)

            def route(l):
                s = L[l]
                v = lambda a: a.rearrange("p a b -> p (a b)")
                b16 = lambda a: wide(a.unsqueeze(1), [P, 5, NE])
                over = lambda a: wide(a.unsqueeze(2), [P, 5, NE])
                over4 = lambda a: wide(a.unsqueeze(2), [P, 5, NG])
                g = flat(grp(("ru", l)))
                part = g[:, 0:5 * P].rearrange("p (i j e) -> p i e j", i=5, j=4)[:, :, 0:NE, :]
                dve.tensor_reduce(R["sc"][:, 0:4, :], part[:, 0:4], AX.X, ALU.add)
                dve.tensor_reduce(R["sc"][0:NS, 4:5, :], part[0:NS, 4:5], AX.X, ALU.add).then_inc(freed, 1)
                settled("logits")
                dve.sem_inc(s["logits_ready"], 1)
                dve.wait_ge(s["scores_ready"], 1)
                link(tt(R["sel"], R["sc"], b16(rbias[:, :]), ALU.add))
                x = v(R["sel"]).rearrange("p (a b) -> p a b", b=2)
                tt(hi, x[:, :, 0], x[:, :, 1], ALU.max)
                link(tt(lo, x[:, :, 0], x[:, :, 1], ALU.min))
                hh, ll = (a.rearrange("p (a b) -> p a b", b=2) for a in (hi, lo))
                top1, m2, l2, gs, e4, c4_, ing, inb = (v(R4[n]) for n in "top1 m2 l2 gs e4 c4 ing inb".split())
                tt(top1, hh[:, :, 0], hh[:, :, 1], ALU.max)
                tt(m2, hh[:, :, 0], hh[:, :, 1], ALU.min)
                link(tt(l2, ll[:, :, 0], ll[:, :, 1], ALU.max))
                link(tt(m2, m2, l2, ALU.max))
                link(tt(gs, top1, m2, ALU.add))
                link(dve.tensor_reduce(R5["v1"], R4["gs"], AX.X, ALU.max))
                link(tt(R4["e4"], R4["gs"], over4(R5["v1"]), ALU.is_equal))
                link(tt(R4["c4"], R4["e4"], wide(cst("rev4").unsqueeze(1), [P, 5, NG]), ALU.mult))
                link(dve.tensor_reduce(R5["m"], R4["c4"], AX.X, ALU.max))
                link(tt(R4["ing"], R4["c4"], over4(R5["m"]), ALU.is_equal))
                link(ts(inb, ing, -1.0, 1e30, ALU.add, ALU.mult))
                q4 = lambda a: v(a).rearrange("p (a b) -> p a b", b=EG)
                w4 = lambda a: wide(a.unsqueeze(2), [P, 20, EG])
                link(tt(q4(R["a"]), q4(R["sel"]), w4(ing), ALU.mult))
                link(tt(q4(R["a"]), q4(R["a"]), w4(inb), ALU.add))
                for n, src in (("oh1", "a"), ("oh2", "b")):
                    link(dve.tensor_reduce(R5["v1"], R[src], AX.X, ALU.max))
                    link(tt(R["t"], R[src], over(R5["v1"]), ALU.is_equal))
                    link(tt(R["t"], R["t"], b16(cst("rev16")), ALU.mult))
                    link(dve.tensor_reduce(R5["m"], R["t"], AX.X, ALU.max))
                    link(tt(R[n], R["t"], over(R5["m"]), ALU.is_equal))
                    if n == "oh1":
                        link(stt(v(R["b"]), v(R["oh1"]), -3e38, v(R["a"]), ALU.mult, ALU.add))
                link(tt(R["M"], R["oh1"], R["oh2"], ALU.add))
                tt(R["M"], R["M"], over(cst("valid")), ALU.mult).then_inc(s["mask_ready"], 1)
                for n, o in (("s1", "oh1"), ("s2", "oh2")):
                    link(tt(R["t"], R["sc"], R[o], ALU.mult))
                    link(dve.tensor_reduce(R5[n], R["t"], AX.X, ALU.add))
                link(tt(R5["dsum"], R5["s1"], R5["s2"], ALU.add))
                link(dve.reciprocal(R5["dsum"], R5["dsum"]))
                tt(R5["w1"], R5["s1"], R5["dsum"], ALU.mult)
                tt(R5["w2"], R5["s2"], R5["dsum"], ALU.mult)

            def place(l):
                s = L[l]
                v = lambda a: a.rearrange("p a b -> p (a b)")
                b16 = lambda a: wide(a.unsqueeze(1), [P, 5, NE])
                g = flat(grp(("cnt", l)))
                dve.tensor_copy(v(R["pos"]), g[:, 0:5 * NE])
                dve.tensor_copy(v(R["t"]), g[:, 512:512 + 5 * NE]).then_inc(freed, 1)
                settled("cnt")
                for i in range(1, 5):
                    link(tt(R["t"][:, i, :], R["t"][:, i, :], R["t"][:, i - 1, :], ALU.add))
                dve.tensor_copy(cnt, R["t"][:, 4, :])
                link(tt(R["pos"][:, 1:5, :], R["pos"][:, 1:5, :], R["t"][:, 0:4, :], ALU.add))
                link(ts(ov, cnt, float(MAIN), None, ALU.is_gt))
                for n in range(2, 5):
                    link(stt(ov, cnt, float(MAIN * n), ov, ALU.is_gt, ALU.add))
                a, b = ov, ova
                for st in (1, 2, 4, 8):
                    dve.tensor_copy(b[:, 0:st], a[:, 0:st])
                    link(tt(b[:, st:NE], a[:, st:NE], a[:, 0:NE - st], ALU.add))
                    a, b = b, (ovb if b is ova else ova)
                run = a
                tt(dlt, run, ov, ALU.subtract)
                link(ts(base16, cst("iota16"), float(P), None, ALU.mult))
                link(tt(dlt, dlt, cst("iota16"), ALU.subtract))
                link(ts(dlt, dlt, float(NE - 1), float(P), ALU.add, ALU.mult))
                link(ts(v(R["t"]), v(R["pos"]), float(MAIN), None, ALU.is_ge))
                link(tt(R["t"], R["t"], b16(dlt), ALU.mult))
                link(tt(R["slot"], R["pos"], b16(base16), ALU.add))
                link(tt(R["slot"], R["slot"], R["t"], ALU.add))
                for j, o in enumerate(("oh1", "oh2")):
                    link(tt(R["t"], R["slot"], R[o], ALU.mult))
                    link(dve.tensor_reduce(R5["m"], R["t"], AX.X, ALU.add))
                    link(dve.tensor_copy(didx[:, j, :], R5["m"]))
                link(tt(cmp8[0:1], wide(run[0:1].unsqueeze(1), [1, 8, NE]),
                        wide(cst("iota8")[0:1].unsqueeze(2), [1, 8, NE]), ALU.is_le))
                link(dve.tensor_reduce(nb8[0:1, :], cmp8[0:1], AX.X, ALU.add))
                ts(bex[0:1, NE:MAXBLK], nb8[0:1, :], float(NE - 1), None, ALU.min)
                dve.tensor_copy(bex[0:1, 0:NE], cst("iota16")[0:1, :])
                link(ts(nit[0:1, 0:1], run[0:1, NE - 1:NE], 0.0, float(NE // 2), ALU.is_gt, ALU.add))
                for n in (2, 4, 6):
                    link(stt(nit[0:1, 0:1], run[0:1, NE - 1:NE], float(n), nit[0:1, 0:1], ALU.is_gt, ALU.add))
                link(dve.tensor_copy(bexp[0:1, :], bex[0:1, :]))
                dve.tensor_copy(niter[0:1, 0:1], nit[0:1, 0:1]).then_inc(s["route_ready"], 1)

            def moe(l):
                s = L[l]
                if l == 0:
                    dve.wait_ge(z_out, 16 * 2 * (MAXBLK - NE))
                    dve.wait_ge(st_out, 16 * RH)
                dve.memset(v_sc := R["sc"].rearrange("p a b -> p (a b)"), 0.5).then_inc(s["sc_zeroed"], 1)
                dve.memset(tabz, 0.0).then_inc(s["tab_zero"], 1)
                norm(1 + 3 * l, 48 * l + 24, G_FFN + 8 * l)
                route(l)
                for f in range(FT):
                    g = grp(("su", l, f))
                    act_took(("sg", l, f))
                    tt(shT[:, f, :, :], xw(g), sgs, ALU.mult).then_inc(freed, 1)
                    settled("sh")
                    dve.sem_inc(s["shT_ready"], 1)
                place(l)
                for t in range(DT):
                    residual(("sd", l, t), t, 48 * l + 40)
                g = flat(grp(("ix", l)))
                dve.tensor_copy(idx[:, :], g[:, 0:TABLE]).then_inc(freed, 1)
                psY = PS[:, 5:7, :].rearrange("p a b -> p (a b)")

                def block_of(it, u, first):
                    b = it * 2 + u
                    dve.wait_ge(s["sg_ready"], b + 1)
                    dve.wait_ge(s["gu_done"], b + 1)
                    tt(hid, sg, PS[:, 3, :], ALU.mult).then_inc(s["hid_ready"], 1)
                    dve.wait_ge(s["ht_done"], b + 1)
                    dve.tensor_copy(hidT.rearrange("p a b -> p (a b)"), PS[:, 4, :]).then_inc(s["hidT_ready"], 1)
                    dve.wait_ge(s["y_done"], b + 1)
                    if not first:
                        dve.wait_ge(s["stored"][u], it * 16)
                    dve.tensor_copy(ysb[u], psY).then_inc(s["yout_ready"], 1)

                dve.wait_ge(s["rows_out"][0], 48)
                dve.wait_ge(s["rows_out"][1], 32)
                block_of(0, 0, True)
                block_of(0, 1, True)
                dve.wait_ge(s["route_ready"], 1)
                n_it = dve.value_load(niter[0:1, 0:1], min_val=8, max_val=MAXBLK // 2)
                with dve.Fori(1, n_it) as it:
                    for u in range(2):
                        block_of(it, u, False)
                dve.sem_inc(s["loop_end"], 1)
                dve.wait_ge(s["hb_ready"], n_it * 2 + 1)
                gate = 48 * l + 40
                for i in range(5):
                    n = P if i < 4 else NS
                    ga, gb = (hblk[0], hblk[1]) if i % 2 == 0 else (ysb[0], ysb[1])
                    dve.wait_ge(s["got"][2 * (i % 2)], 16 * (i // 2 + 1))
                    dve.wait_ge(s["got"][2 * (i % 2) + 1], 16 * (i // 2 + 1))
                    out = hbT[i % 2].rearrange("p t n -> p (t n)")
                    link(ts(out[0:n, :], ga[0:n, :], R5["w1"][0:n, i:i + 1], None, ALU.mult))
                    stt(out[0:n, :], gb[0:n, :], R5["w2"][0:n, i:i + 1], out[0:n, :],
                        ALU.mult, ALU.add).then_inc(s["comb_ready"], 1)
                    if i:
                        add_back(l, i - 1, gate)
                add_back(l, 4, gate)

            def add_back(l, i, gate):
                g = flat(grp(("cb", l, i)))
                src = g.rearrange("p (t n) -> p t n", t=DT)
                if i < 4:
                    for t in range(DT):
                        xs = xT[:, t, i // 2, (i % 2) * P:(i % 2) * P + P]
                        last = stt(xs, src[:, t, :], mod[:, gate + t, 0:1], xs, ALU.mult, ALU.add)
                    last.then_inc(freed, 1)
                else:
                    t8 = sg[:, 0:DT * NS].rearrange("p (t n) -> p t n", t=DT)
                    link(tt(t8, src[:, :, 0:NS], mod[:, gate:gate + DT, 1:NSEQ], ALU.mult))
                    xs = xT[:, :, :, HP:HALF]
                    tt(xs, xs, t8.rearrange("p t (a b) -> p t a b", a=2), ALU.add).then_inc(freed, 1)
                settled("x")
                dve.sem_inc(x_updated, 1)
                xup[0] += 1

            moe(0)

            norm(2, 96, G_KV)
            act_took("zk")
            g = grp("kr")
            tt(mt[0][0:ROPE], xw(g)[0:ROPE], sinm[0:ROPE], ALU.mult).then_inc(freed, 1)
            link(tt(mt[1][0:ROPE], zk[0:ROPE], cosm[0:ROPE], ALU.mult))
            tt(two(kpeT[0:ROPE, 0:NP]), mt[1][0:ROPE, :, 0:HP], mt[0][0:ROPE, :, 0:HP], ALU.add)
            tt(two(kpeT[0:ROPE, NP:T]), mt[1][0:ROPE, :, HP:HALF], mt[0][0:ROPE, :, HP:HALF],
               ALU.add).then_inc(kpe_ready, 1)
            act_took("zss")
            link(dve.reciprocal(rs[:, :, :], rs[:, :, :]))
            for t in range(2):
                gc = cols[:, N_BIAS + G_CKV + t:N_BIAS + G_CKV + t + 1]
                stt(two(ckvT[:, t, 0:NP]), zT[:, t, :, 0:HP], gc, rs[:, :, 0:HP], ALU.mult, ALU.mult)
                last = stt(two(ckvT[:, t, NP:T]), zT[:, t, :, HP:HALF], gc, rs[:, :, HP:HALF], ALU.mult, ALU.mult)
            last.then_inc(ckv_ready, 1)
            dve.memset(qsl.rearrange("p a b c -> p (a b c)"), 0.0)

            norm(3, 48, G_MIX + 8)
            act_took("qss")
            link(dve.reciprocal(rs[:, :, :], rs[:, :, :]))
            for t in range(2):
                gc = cols[:, N_BIAS + G_CQ + t:N_BIAS + G_CQ + t + 1]
                last = stt(cqT[:, t, :, :], zT[:, t, :, :], gc, rs[:, :, :], ALU.mult, ALU.mult)
            last.then_inc(cq_ready, 1)

            def query(h):
                for t in range(2):
                    g = grp(("ql", h, t))
                    dve.tensor_copy(two(ql[:, t, 0:NP]), g[:, :, 0:HP])
                    last = dve.tensor_copy(smp(qsl[:, t, :, h]), g[:, :, HP:HALF])
                    last.then_inc(freed, 1)
                settled("ql")
                dve.sem_inc(ql_ready, 1)
                g = grp(("qr", h))
                tt(qt[0][0:ROPE], xw(g)[0:ROPE], sinm[0:ROPE], ALU.mult).then_inc(freed, 1)
                link(tt(qt[1][0:ROPE], qpr[0:ROPE], cosm[0:ROPE], ALU.mult))
                settled("qr")
                tt(two(qpe[0:ROPE, 0:NP]), qt[1][0:ROPE, :, 0:HP], qt[0][0:ROPE, :, 0:HP], ALU.add)
                tt(smp(qsl[0:ROPE, 2, :, h]), qt[1][0:ROPE, :, HP:HALF], qt[0][0:ROPE, :, HP:HALF],
                   ALU.add).then_inc(qpe_ready, 1)

            query(0)
            for h in range(MH):
                for name, chunks in SCORES:
                    n = group_no[(name, h)]
                    dve.wait_ge(group_done, n + 1)
                    g = flat(pair(n))
                    for i, at in chunks:
                        d = g[:, at + i * P:at + (i + 1) * P]
                        last = tt(d, d, cst("causal"), ALU.add)
                    link(last)
                    for i, at in chunks:
                        last = dve.tensor_reduce(mcol[:, i:i + 1], g[:, at:at + (i + 1) * P], AX.X, ALU.max)
                link(last)
                ts(mcol[:, 4:8], mcol[:, 0:4], -MLA_SCALE, None, ALU.mult).then_inc(mx_ready, 1)
                act_took(("sb_mla", h))
                link(dve.reciprocal(mcol[:, 12:16], mcol[:, 8:12]))
                for i in range(4):
                    c = pr_[:, TRI[i]:TRI[i + 1]]
                    last = ts(c, c, mcol[:, 12 + i:13 + i], None, ALU.mult)
                last.then_inc(p_ready, 1)
                if h + 1 < MH:
                    act_took(("qp", h + 1))
                    query(h + 1)
                g = grp(("ol", h))
                dve.tensor_copy(olat, g).then_inc(freed, 1)

            for q in range(2):
                for j in range(4):
                    b = 4 * q + j
                    for t in (0, 2):
                        m = P if t < 2 else ROPE
                        g = flat(grp(("kt3", b, t)))
                        dve.tensor_copy(KT[0:m, t, :], g[0:m, :]).then_inc(freed, 1)
                    g = flat(grp(("sp", b)))
                    for c in range(4):
                        last = dve.tensor_copy(S_sb[32 * j:32 * j + 32, c * 256:(c + 1) * 256],
                                               g[32 * c:32 * c + 32, 0:256])
                    last.then_inc(freed, 1)
                new = lambda a: wide(a[:, NP + 4 * q:NP + 4 * q + 4].unsqueeze(2), [a.shape[0], 4, 32])
                for t in range(3):
                    m, k = (P, ckvT[:, t, :]) if t < 2 else (ROPE, kpeT[0:ROPE, :])
                    last = tt(prodn[0:m, t, :].rearrange("p (a b) -> p a b", a=4), qsl[0:m, t, 4 * q:4 * q + 4, :],
                              new(k), ALU.mult)
                last.then_inc(prodn_ready, 1)
                g = flat(grp(("sn", q)))
                dve.tensor_copy(S_sb[:, PAST:PAST + 1], g[:, 0:1]).then_inc(freed, 1)
                settled("S")
                link(dve.tensor_reduce(mcol2[:, 0:1], S_sb, AX.X, ALU.max))
                ts(mcol2[:, 1:2], mcol2[:, 0:1], -MLA_SCALE, None, ALU.mult).then_inc(smx_ready, 1)
                dve.wait_ge(se_ready, q + 1)
                link(dve.reciprocal(mcol2[:, 3:4], mcol2[:, 2:3]))
                ts(Ps, Ps, mcol2[:, 3:4], None, ALU.mult).then_inc(sp_ready, 1)
                g = grp(("pv", q))
                dve.wait_ge(sp_ready, q + 1)
                link(ts(onew, g[:, 1, 0:LAT], Ps[:, PAST:PAST + 1], None, ALU.mult))
                tt(olr, g[:, 0, 0:LAT], onew, ALU.add).then_inc(freed, 1)
                settled("olr")
                dve.sem_inc(olr_ready, 1)
                g = flat(grp(("olt", q)))
                for t in range(2):
                    last = dve.tensor_copy(osl[:, t, 4 * q:4 * q + 4, :],
                                           g[:, t * P:(t + 1) * P].rearrange("p (a b) -> p a b", a=4)[:, :, 0:MH])
                last.then_inc(freed, 1)
            for t in range(DT):
                residual(("mo", t), t, 48 + 16)
            moe(1)
            norm(5, 0, G_FIN, modulated=False)

        @block.gpsimd
        def _(pool):
            def moe(l):
                s = L[l]
                pool.wait_ge(s["tab_zero"], 1)
                pool.dma_start(t_dram[l].rearrange("(a b) c -> a (b c)", b=P), tabz[0:TABLE, :]).then_inc(s["tab_zeroed"], 16)
                pool.wait_ge(s["tab_zeroed"], 16)
                pool.wait_ge(s["route_ready"], 1)
                for i in range(5):
                    n = P if i < 4 else NS
                    for j in range(2):
                        pool.indirect_dma_start(
                            out=t_dram[l], out_offset=bass.IndirectOffsetOnAxis(ap=didx[0:n, j, i:i + 1], axis=0),
                            in_=cst("tokid")[0:n, i:i + 1], in_offset=None).then_inc(s["scattered"], 16)
                pool.wait_ge(s["scattered"], 160)
                pool.dma_start(tabr[0:TABLE, :], t_dram[l].rearrange("(a b) c -> a (b c)", b=P)).then_inc(s["tab_in"], 16)
                n_ix, c_ix = group_who[group_no[("ix", l)]]
                pool.wait_ge(took[n_ix], c_ix)
                pool.wait_ge(s["rows_out"][0], 48)
                pool.wait_ge(s["rows_out"][1], 32)

                def gather(b, u, nth):
                    pool.tensor_copy(idxc[:, u:u + 1], idx[:, b:b + 1] if isinstance(b, int) else
                                     idx[:, bass.ds(b, 1)]).then_inc(s["idxc_ready"], 1)
                    pool.wait_ge(s["idxc_ready"], nth)
                    pool.sem_inc(s["idxc_seen"], 1)
                    pool.indirect_dma_start(
                        out=hblk[u], out_offset=None, in_=h_dram[l],
                        in_offset=bass.IndirectOffsetOnAxis(ap=idxc[:, u:u + 1], axis=0)).then_inc(s["gathered"][u], 16)

                def store(b, u, need):
                    pool.wait_ge(s["yout_ready"], need)
                    rows = y_dram.rearrange("(b p) d -> b p d", p=P)
                    dst = rows[b] if isinstance(b, int) else rows[bass.ds(b, 1)].rearrange("a p d -> p (a d)")
                    pool.dma_start(dst, ysb[u]).then_inc(s["stored"][u], 16)

                gather(0, 0, 1)
                gather(1, 1, 2)
                n_it = pool.value_load(niter[0:1, 0:1], min_val=8, max_val=MAXBLK // 2)

                def turn(it, n0, last):
                    for u in range(2):
                        b = it * 2 + u
                        if not (last and u):
                            pool.wait_ge(s["th_done"], b + 1)
                            pool.wait_ge(s["gathered"][u], it * 16 + 16)
                            gather(b + 2, u, b + 3)
                        store(b, u, b + 1)

                turn(0, n_it, False)
                with pool.Fori(1, n_it) as it:
                    turn(it, n_it, False)
                pool.wait_ge(s["gathered"][0], n_it * 16 + 16)
                pool.wait_ge(s["gathered"][1], n_it * 16 + 16)
                pool.wait_ge(s["stored"][0], n_it * 16)
                pool.wait_ge(s["stored"][1], n_it * 16)
                pool.wait_ge(s["th_done"], n_it * 2 + 1)
                pool.sem_inc(s["idxc_seen"], 1)
                for i in range(5):
                    n = P if i < 4 else NS
                    dst = (hblk[0], hblk[1]) if i % 2 == 0 else (ysb[0], ysb[1])
                    if i >= 2:
                        pool.wait_ge(s["comb_ready"], i - 1)
                    for j in range(2):
                        pool.indirect_dma_start(
                            out=dst[j][0:n, :], out_offset=None, in_=y_dram,
                            in_offset=bass.IndirectOffsetOnAxis(ap=didx[0:n, j, i:i + 1], axis=0)
                        ).then_inc(s["got"][2 * (i % 2) + j], 16)

            pool.wait_ge(z_ready, 1)
            for b in range(NE, MAXBLK):
                for c in range(2):
                    pool.dma_start(y_dram[b * P:(b + 1) * P, c * 512:(c + 1) * 512], ztile).then_inc(z_out, 16)
            pool.wait_ge(z_out, 16 * 2 * (MAXBLK - NE))
            moe(0)
            moe(1)

        @block.sync
        def _(sp):
            sp.dma_start(xrows[:, 0:4, :], A["x_prompt"][0].rearrange("(i p) d -> p i d", p=P)).then_inc(s_x, 16)
            sp.dma_start(xrows[0:NS, 4, :], A["x_sample"].rearrange("b a d -> (b a) d")).then_inc(s_x, 16)
            sp.dma_start(rbrow[0:1, :], A["router_bias"].rearrange("(a e) -> a e", a=1)).then_inc(s_rb, 16)
            sp.wait_ge(rw_zeroed, 1)
            sp.dma_start(rw[:, :, 0:NE], A["router_w"].rearrange("(t p) e -> p t e", p=P)).then_inc(s_rw, 16)
            sp.dma_start(ptab[0:1, :], A["page_table"].rearrange("(x a) b -> x (a b)", x=1)).then_inc(s_pt, 16)

            def experts(l):
                s = L[l]
                base = s["base"]
                srcs = (A["moe_w_gate"][l], A["moe_w_up"][l], A["moe_w_down"][l])
                n_it = None

                def fetch(e, u, j):
                    w = W[:, (base + 3 * u + j) % 6, :].rearrange("p (t n) -> p t n", n=(FE, FE, D)[j])
                    src = srcs[j][e] if isinstance(e, int) else srcs[j][bass.ds(e, 1)].rearrange("a k n -> (a k) n")
                    sp.dma_start(w, src.rearrange("(t p) n -> p t n", p=P)).then_inc(s["w_in"][3 * u + j], 16)

                for u in range(2):
                    for j in range(3):
                        free_slot(s["prior"] + 3 * u + j)
                        fetch(u, u, j)
                sp.wait_ge(s["route_ready"], 1)
                n_it = sp.value_load(niter[0:1, 0:1], min_val=8, max_val=MAXBLK // 2)
                with sp.Fori(1, n_it) as it:
                    for u in range(2):
                        b = it * 2 + u
                        e = sp.value_load(bexp[0:1, bass.ds(b, 1)], min_val=0, max_val=NE - 1)
                        sp.wait_ge(s["gu_done"], b - 1)
                        fetch(e, u, 0)
                        fetch(e, u, 1)
                        sp.wait_ge(s["y_done"], b - 1)
                        fetch(e, u, 2)
                sp.wait_ge(s["loop_end"], 1)

            def free_slot(k):
                if k < 6 or (k - 6) < expert_floor[0]:
                    return
                name = loads[k - 6][0]
                sp.wait_ge(group_done, last_group[k - 6])
                if name[0] == "S":
                    sp.wait_ge(ss_out[name[1]], 32)

            expert_floor = [0]
            done_moe = 0
            for k, (name, slot, parts) in enumerate(loads):
                if done_moe < 2 and k == L[done_moe]["prior"]:
                    experts(done_moe)
                    done_moe += 1
                    expert_floor[0] = k
                free_slot(k)
                w = W[:, slot, :]
                if parts is not None:
                    for dst, src in parts:
                        sp.dma_start(dst(w), src).then_inc(slot_in[slot], 16)
                else:
                    b = name[1]
                    pg_view = w[:, 0:NPAGE * (LAT + ROPE)]
                    if b == 0:
                        sp.wait_ge(s_pt, 16)
                    with sp.Fori(0, NPAGE) as pg:
                        page = sp.value_load(ptab[0:1, bass.ds(pg + b * NPAGE, 1)], min_val=0,
                                             max_val=A["cache_ckv"].shape[0] - 1)
                        sp.dma_start(pg_view[:, bass.ds(pg * (LAT + ROPE), LAT)],
                                     A["cache_ckv"][bass.ds(page, 1)].rearrange("a p c -> p (a c)")
                                     ).then_inc(slot_in[slot], 16)
                        sp.dma_start(pg_view[:, bass.ds(pg * (LAT + ROPE) + LAT, ROPE)],
                                     A["cache_kpe"][bass.ds(page, 1)].rearrange("a p c -> p (a c)")
                                     ).then_inc(slot_in[slot], 16)
            while done_moe < 2:
                experts(done_moe)
                done_moe += 1


_INS = ["x_prompt", "x_sample", "c_prompt", "c_sample", "state_ret", "cache_ckv", "cache_kpe", "page_table",
        "w_ada", "b_ada", "norm_mix_g", "norm_ffn_g", "ret_w_in", "ret_gn_g", "ret_w_out", "kv_w_ada", "kv_b_ada",
        "kv_norm_g", "mla_w_dkv", "mla_kv_norm_g", "mla_w_uk", "mla_w_uv", "mla_w_dq", "mla_q_norm_g", "mla_w_uq",
        "mla_w_o", "router_w", "router_bias", "moe_w_gate", "moe_w_up", "moe_w_down", "shared_w_gate",
        "shared_w_up", "shared_w_down", "final_norm_g"]
_OUTS = [("y_p", (1, NP, D)), ("y_s", (NS, 1, D)), ("state_p", (1, 1, RH, RD, RD)), ("state_s", (1, NS, RH, RD, RD)),
         ("ckv_p", (1, NP, LAT)), ("kpe_p", (1, NP, ROPE)), ("ckv_s", (NS, 1, LAT)), ("kpe_s", (NS, 1, ROPE))]


def kernel(**inputs):
    import concourse.bacc as _bacc
    from concourse.bass_utils import run_bass_kernel_spmd as _run

    nc = _bacc.Bacc("TRN2", target_bir_lowering=False, num_devices=1)
    arrays, ins, outs = {}, {}, {}
    for name in _INS:
        arrays[name] = np.ascontiguousarray(inputs[name])
    arrays["tables"] = shape_tables()
    for name, a in arrays.items():
        ins[name] = nc.dram_tensor(name, a.shape, mybir.dt.from_np(a.dtype), kind="ExternalInput").ap()
    for name, shape in _OUTS:
        outs[name] = nc.dram_tensor("out_" + name, shape, F32, kind="ExternalOutput").ap()
    build(nc, ins, outs)
    r = _run(nc, [arrays], core_ids=[0])
    return tuple(r.results[0]["out_" + name] for name, _ in _OUTS)
```

```python
from contextlib import ExitStack

import numpy as np

import concourse.bass as bass
from concourse import mybir

F32 = mybir.dt.float32
I32 = mybir.dt.int32
ALU = mybir.AluOpType
ACT = mybir.ActivationFunctionType
AX = mybir.AxisListType

P = 128
D = 1024
DT = D // P
NP, NS = 512, 8
HALF, HP, HS = 260, 256, 4
T = NP + NS
PAST = 1024
RH, RD = 4, 256
MH, NOPE, ROPE, LAT = 8, 128, 64, 256
NE, NG, EG = 16, 4, 4
FE = 512
FT = FE // P
PAGE, NPAGE = 128, 8
MLA_SCALE = (NOPE + ROPE) ** -0.5
EPS = 1e-6
NSEQ = 1 + NS
TAILS, TAIL_SEQ = (2, 3), 6
TAIL_PAGES = NPAGE // 2
ADA_UNITS = 28
MAXBLK = NE + 2 * T // P
TABLE = MAXBLK + 2
MAIN = P

WIDTHS = [("ident", P), ("ones", P), ("eps", 1), ("inv256", P), ("tri", P), ("decay", RH * NP), ("kdec", RH * 4),
          ("cosr", 2 * HALF), ("sinr", 2 * HALF), ("cosm", 2 * HALF), ("sinm", 2 * HALF), ("rot", ROPE),
          ("causal", P), ("rev16", NE), ("iota16", NE), ("rev4", NG), ("valid", 5), ("tokid", 5),
          ("iota8", 8), ("selq", 2 * P)]
AT, _at = {}, 0
for _n, _w in WIDTHS:
    AT[_n] = (_at, _w)
    _at += _w
CW = _at
FIRST = AT["inv256"][0]

G_MIX, G_FFN, G_KV, G_GN, G_FIN, G_CKV, G_CQ, N_GAIN = 0, 16, 32, 40, 48, 56, 58, 60
N_BIAS = 112


def shape_tables():
    c = np.zeros((P, CW), np.float32)

    def put(name, a):
        s, w = AT[name]
        a = np.asarray(a, np.float32).reshape(-1, w)
        c[:a.shape[0], s:s + w] = a

    p = np.arange(P)
    put("ident", np.eye(P))
    put("ones", np.ones((P, P)))
    put("inv256", np.full((P, P), 1 / RD))
    put("tri", p[:, None] < p[None, :])
    g = 1 - np.exp2(-5.0 - np.arange(RH))
    x = np.arange(NP)
    diff = x[None, None, :] - p[:, None, None]
    put("decay", np.where(diff >= 0, g[None, :, None] ** np.maximum(diff, 0), 0) * RD ** -0.5)
    put("kdec", g[None, :, None] ** (NP - 1 - (P * np.arange(4)[None, None, :] + p[:, None, None])))
    half = np.zeros((2, HALF))
    half[:, :HP] = np.arange(NP).reshape(2, HP)
    half[:, HP:] = PAST
    pos = half.reshape(-1).astype(np.float32)
    for name, d in (("r", RD), ("m", ROPE)):
        inv = np.float32(10000.0) ** (-np.arange(0, d, 2, dtype=np.float32) / np.float32(d))
        if d == ROPE:
            inv = np.tile(inv, 2)
        ang = (pos[None, :] * inv[:, None].astype(np.float32)).astype(np.float64)
        put("cos" + name, np.cos(ang))
        put("sin" + name, np.sin(ang))
    rot = np.zeros((ROPE, ROPE))
    q = np.arange(ROPE // 2)
    rot[q + 32, q] = -1
    rot[q, q + 32] = 1
    put("rot", rot)
    put("causal", np.where(p[None, :] <= p[:, None], 0, -1e30))
    put("rev16", np.tile(NE - np.arange(NE), (P, 1)))
    put("iota16", np.tile(np.arange(NE), (P, 1)))
    put("rev4", np.tile(NG - np.arange(NG), (P, 1)))
    put("valid", np.stack([np.ones(P)] * 4 + [p < NS], 1))
    put("tokid", np.stack([P * i + p for i in range(4)] + [NP + np.minimum(p, NS - 1)], 1))
    put("eps", np.full((P, 1), EPS))
    put("iota8", np.tile(np.arange(8), (P, 1)))
    put("selq", p[:NS, None, None] == 4 * np.arange(2)[None, :, None] + p[None, None, :] // 32)
    return c


def build(nc, A, O):
    ctx = ExitStack()
    with ctx:
        def sb(name, shape, dt=F32):
            return ctx.enter_context(nc.sbuf_tensor(name, shape, dt))

        def sem(name):
            return ctx.enter_context(nc.semaphore(name))

        C = sb("shape_tables_sb", [P, CW])
        xT = sb("xT", [P, DT, 2, HALF])
        hT = sb("hT", [P, DT, 2, HALF])
        hS = sb("h_samples", [P, DT, NS])
        W = sb("wring", [P, 6, 4096])
        mod = sb("mod", [P, N_BIAS, NSEQ])
        cols = sb("cols", [P, N_BIAS + N_GAIN])
        csT = sb("csT", [P, DT, 32])
        apart = sb("apart", [P, 2, T])
        asum = sb("asum", [P, 2, 4 * NSEQ])
        acol = sb("acol", [P, DT, NSEQ])
        rs = sb("rs", [P, 2, HALF])
        rw = sb("rw", [P, DT, 32])
        rbias = sb("rbias", [P, NE])
        tmp8 = sb("tmp8", [P, DT, 2, HS])
        niter = sb("niter", [1, 1], I32)
        bexp = sb("bexp", [1, MAXBLK], I32)
        didx = sb("didx", [P, 2, 5], I32)
        idx = sb("idx", [P, TABLE], I32)
        idxc = sb("idxc", [P, 2], I32)
        ptab = sb("ptab", [1, NS * NPAGE], I32)
        AR = 11450
        arena = sb("arena", [P, AR])
        PS = ctx.enter_context(nc.psum_tensor("PS", [P, 8, 512], F32))

        def cst(name):
            s, w = AT[name]
            return C[:, s:s + w]

        ident, ones, inv256, tri = cst("ident"), cst("ones"), cst("inv256"), cst("tri")
        decay = cst("decay").rearrange("p (h x) -> p h x", h=RH)
        two = lambda a: a.rearrange("p (a b) -> p a b", a=2)
        cosr, sinr, cosm, sinm = (two(cst(n)) for n in ("cosr", "sinr", "cosm", "sinm"))

        class Carve:
            def __init__(self, region, at=0):
                self.region, self.at = region, at

            def __call__(self, *shape):
                n = int(np.prod(shape))
                v = self.region[:, self.at:self.at + n]
                self.at += n
                assert self.at <= self.region.shape[1], self.at
                if len(shape) == 2:
                    v = v.rearrange("p (a b) -> p a b", a=shape[0])
                if len(shape) == 3:
                    v = v.rearrange("p (a b c) -> p a b c", a=shape[0], b=shape[1])
                return v

        c0 = Carve(arena[:, :])
        xrows = c0(5, D)
        crow, csilu = c0(D), c0(D)
        brows, grows = c0(P), c0(P)
        rbrow = c0(NE)
        c1 = Carve(arena[:, :])
        qT, kT = c1(2, T), c1(2, T)
        gT = c1(2, 2, HALF)
        vtok = c1(5, RD)
        PT = [c1(NP - P * j) for j in range(4)]
        kdec = c1(4, RD)
        oT = c1(2, T)
        sq = c1(2, T)
        yT = sq.rearrange("p a b -> p (a b)").rearrange("p (a h b) -> p a h b", a=2, h=2)
        rope_at = c1.at
        rt = [c1(2, HALF) for _ in range(4)]
        kmask = Carve(arena[:, :], rope_at)(NS, RD)
        stout = c1(2, RD)
        ks = Carve(sq.rearrange("p a b -> p (a b)"))(RD)
        osb = Carve(arena[:, :], rope_at)(2, RD)
        rs2 = rs[:, :, :]
        ztile = stout.rearrange("p a b -> p (a b)")
        c2 = Carve(arena[:, :])
        hblk = [c2(D) for _ in range(2)]
        hbT = [c2(DT, P) for _ in range(2)]
        ysb = [c2(D) for _ in range(2)]
        sg = c2(FE)
        sgs_at = c2.at
        hid, hidT = c2(FE), c2(FT, P)
        sgs = Carve(arena[:, :], sgs_at)(2, HALF)
        shT = c2(FT, 2, HALF)
        R = {n: c2(5, NE) for n in "sc sel oh1 oh2 a b M pos slot t".split()}
        R4 = {n: c2(5, NG) for n in "top1 m2 l2 gs e4 c4 ing inb".split()}
        hi, lo = c2(40), c2(40)
        lg, lgs = Carve(arena[:, :])(2, HALF), c2(NS)
        R5 = {n: c2(5) for n in "v1 m s1 s2 w1 w2 dsum".split()}
        cnt, ov, ova, ovb, dlt, base16 = (c2(NE) for _ in range(6))
        cmp8 = c2(8, NE)
        nb8 = c2(8)
        bex = c2(MAXBLK)
        nit = c2(4)
        tabz, tabr = c2(P), c2(P)
        c3 = Carve(arena[:, :])
        ckvT = c3(2, T)
        kpeT = apart[:, 0, :]
        ctok = c3(5, LAT + ROPE)
        cqT = c3(2, 2, HALF)
        uvT = c3(MH, 2, P)
        qsl = c3(3, NS, 32)
        share_at = c3.at
        zT = c3(2, 2, HALF)
        zk = c3(2, HALF)
        qn = c3(2, HALF)
        qpr = c3(2, HALF)
        ql = c3(2, T)
        qpe = apart[:, 1, :]
        pr_ = c3(10 * P)
        mcol = c3(16)
        msq = Carve(arena[:, :], share_at + 4 * 2 * HALF)(2, 2, HALF)
        mt = [qn, Carve(pr_)(2, HALF)]
        qt = [zT[:, t, :, :] for t in range(2)]
        dead = C[:, AT["decay"][0]:AT["decay"][0] + 3104]
        rl = Carve(dead)(2, HALF)
        c4 = Carve(dead)
        PTm = c4(4, NP)
        olat = c4(2, NP)
        KT = Carve(dead)(3, NPAGE * PAGE)
        c5 = Carve(arena[:, :], share_at)
        S_sb = [c5(PAST + 1), cqT.rearrange("p a b c -> p (a b c)")[:, 0:PAST + 1]]
        Ps = c5(PAST + 1)
        PTs = c5(NPAGE, P)
        prodn = c5(3, P)
        onew, olr = c5(LAT), c5(LAT)
        osl = c5(2, NS, MH)
        mcol2 = c5(4)
        TRI = [P * i * (i + 1) // 2 for i in range(5)]
        SCORES = (("sa", ((0, 0), (1, P), (2, 512))), ("sb", ((3, 0),)))
        SCORES = tuple((n + "_mla", c) for n, c in SCORES)
        TURNS = (("pta", ((0, 0), (1, P), (2, 3 * P))), ("ptb", ((3, 0),)))
        orow = [Carve(arena[:, :], 0)(D), Carve(arena[:, :], D)(D)]

        h_dram = [nc.dram_tensor(f"h_rows{l}", (T, D), F32, kind="Internal").ap() for l in range(2)]
        y_dram = nc.dram_tensor("y_rows", (MAXBLK * P, D), F32, kind="Internal").ap()
        t_dram = [nc.dram_tensor(f"slot_table{l}", (TABLE * P, 1), F32, kind="Internal").ap() for l in range(2)]

        s_tab, s_tab2, s_rows, s_c, s_x, s_rw = (sem(n) for n in ("set_up_tables_in", "tables_in", "rows_in", "c_in", "x_in", "router_in"))
        s_pt, s_rb = sem("page_table_in"), sem("router_bias_in")
        slot_in = [sem(f"slot_in{i}") for i in range(6)]
        group_done = sem("group_done")
        took = {"dve": sem("dve_took_group"), "act": sem("act_took_group")}
        dve_chain = sem("dve_chain")
        cs_zeroed, rw_zeroed, ada_ready = sem("cs_zeroed"), sem("rw_zeroed"), sem("ada_ready")
        csilu_ready, x_updated = sem("csilu_ready"), sem("x_updated")
        sq_ready, h_scaled, h_ready, hs_ready = (
            sem(n) for n in ("squares_ready", "h_scaled", "h_ready", "h_sample_ready"))
        q_ready, k_ready, km_ready, st_updated, o_ready, oc_ready, osq_ready, y_ready = (
            sem(n) for n in ("q_ready", "k_ready", "kmask_ready", "states_updated", "o_ready", "o_centered",
                             "o_squared", "y_ready"))
        st_out, ss_out = sem("state_p_out"), [sem(f"state_s_out{i}") for i in range(RH)]
        z_ready, z_out = sem("zeros_ready"), sem("zeros_out")
        outs_done = sem("latents_out")
        L = []
        for l in range(2):
            names = ("sc_filled logits_ready scores_ready mask_ready shT_ready route_ready tab_zero tab_zeroed scattered tab_in "
                     "th_done w_used ht_done hb_ready sg_ready hid_ready hidT_ready yout_ready first_weighted "
                     "idxc_ready idxc_seen comb_ready").split()
            d = {n: sem(f"{n}_{l}") for n in names}
            for n, k in (("rows_out", 2), ("w_in", 6), ("gathered", 2), ("stored", 2), ("got", 10)):
                d[n] = [sem(f"{n}{i}_{l}") for i in range(k)]
            L.append(d)
        msq_ready, ckv_ready, kpe_ready, cq_ready = (
            sem(n) for n in ("latent_squares_ready", "ckv_ready", "kpe_ready", "cq_ready"))
        ql_ready, qpe_ready, mx_ready, p_ready = (
            sem(n) for n in ("q_lat_ready", "q_pe_ready", "max_ready", "p_ready"))
        prodn_ready, smx_ready, se_ready, sp_ready, olr_ready = (
            sem(n) for n in ("new_products_ready", "s_max_ready", "s_exp_ready", "s_p_ready", "o_lat_ready"))
        kpe_in = [sem(f"kpe_pages_in{b}") for b in range(NS)]
        orow_out = [sem(f"y_rows_out{i}") for i in range(2)]

        group_no, group_who, freed_by = {}, [], {"dve": 0, "act": 0}
        loads, load_no, landed, last_group, slot_count = [], {}, {}, {}, [0] * 6

        def pair(n):
            return PS[:, 2 * (n % 4):2 * (n % 4) + 2, :]

        def flat(g):
            return g.rearrange("p a b -> p (a b)")

        def xw(g):
            return g[:, :, 0:HALF]

        def smp(a):
            return a.rearrange("p (a b) -> p a b", a=2)

        def states(w):
            return w.rearrange("p (b t v) -> p b t v", b=NS, t=2)

        def state_rows(dram, h, t):
            return dram[0, :, h, t * P:(t + 1) * P, :].rearrange("b p v -> p b v")

        def h_tile(t, i):
            return hT[:, t, i // 2, (i % 2) * P:(i % 2) * P + P] if i < 4 else hS[:, t, :]

        def y_pair(l, i):
            if i < 2:
                return (hblk, ysb)[i]
            w = W[:, (L[l]["base"] + i - 1) % 6, :]
            return w[:, 0:D], w[:, D:2 * D]

        block = ctx.enter_context(nc.Block())

        @block.tensor
        def _(pe):
            def claim(name, who):
                n = len(group_who)
                group_no[name] = n
                if n >= 4:
                    w, c = group_who[n - 4]
                    pe.wait_ge(took[w], c)
                freed_by[who] += 1
                group_who.append((who, freed_by[who]))
                return pair(n)

            def taken(name):
                w, c = group_who[group_no[name]]
                pe.wait_ge(took[w], c)

            def load(name, parts):
                k = len(loads)
                load_no[name] = k
                slot = k % 6
                loads.append((name, slot, parts))
                slot_count[slot] += 16 * (len(parts) if parts else NPAGE + TAIL_PAGES * (name[1] in TAILS))
                landed[name] = slot_count[slot]
                pe.wait_ge(slot_in[slot], slot_count[slot])
                return W[:, slot, :]

            def used(name):
                last_group[load_no[name]] = len(group_who)

            def mm(out, lhsT, rhs, start=True, stop=True):
                return pe.matmul(out, lhsT=lhsT, rhs=rhs, start=start, stop=stop)

            def project(name, who, lhs, rhs, m=P):
                g = claim(name, who)
                for a in range(2):
                    for k in range(len(lhs)):
                        if rhs is h_all:
                            need_h(a, k)
                        last = mm(g[0:m, a, 0:HALF], lhs[k], rhs[k][:, a, :], k == 0, k == len(lhs) - 1)
                last.then_inc(group_done, 1)

            def w3(w, t, n):
                return w[:, 0:t * n].rearrange("p (t n) -> p t n", t=t)

            ktile = lambda a: a.rearrange("(t p) n -> p t n", p=P)

            def ada_sum(u):
                src = A["w_ada"][u // 12][:, (u % 12) * 512:(u % 12) * 512 + 512] if u < 24 else \
                    A["kv_w_ada"][:, (u - 24) * 512:(u - 24) * 512 + 512]
                w = w3(load(("ada", u), [(lambda w: w3(w, DT, 512), ktile(src))]), DT, 512)
                g = flat(claim(("ada", u), "act"))
                for k in range(DT):
                    j = k % 4
                    last = mm(g[32 * j:32 * j + 32, 0:512], csT[:, k, :], w[:, k, :], k < 4, k >= 4)
                last.then_inc(group_done, 1)
                used(("ada", u))

            def ada_turn(u):
                taken(("ada", u))
                g = flat(claim(("at", u), "dve"))
                for c in range(4):
                    last = pe.transpose(g[:, c * P:(c + 1) * P], apart[:, u % 2, c * P:(c + 1) * P], ident)
                last.then_inc(group_done, 1)

            ada_next, ada_turned = [0], [0]

            def turn_up_to(u):
                while ada_turned[0] < u:
                    ada_turn(ada_turned[0])
                    ada_turned[0] += 1

            def fill(n=1):
                for _ in range(n):
                    u = ada_next[0]
                    ada_next[0] += 1
                    if u < ADA_UNITS:
                        ada_sum(u)
                    turn_up_to(min(u, ADA_UNITS))

            def norm_sum(k):
                g = claim(("ss", k), "act")
                for t in range(DT):
                    pe.wait_ge(sq_ready, (k - (k > 3)) * DT + t + 1)
                    for a in range(2):
                        last = mm(g[:, a, 0:HALF], ones, hT[:, t, a, :], t == 0, t == DT - 1)
                last.then_inc(group_done, 1)

            h_seen = [0, 2 * DT]

            def wait_h(k):
                pe.wait_ge(hs_ready, k + 1)
                h_seen[:] = [k, 0]

            def need_h(a, t):
                if h_seen[1] <= a * DT + t:
                    h_seen[1] = a * DT + t + 1
                    pe.wait_ge(h_ready, h_seen[0] * 2 * DT + h_seen[1])

            h_all = [hT[:, t, :, :] for t in range(DT)]

            pe.wait_ge(s_tab, 16)
            pe.wait_ge(s_x, 32)
            for i in range(5):
                g = flat(claim(("x", i), "dve"))
                n = P if i < 4 else NS
                for t in range(DT):
                    last = pe.transpose(g[:, t * P:t * P + n], xrows[0:n, i, t * P:(t + 1) * P], ident[0:n, 0:n])
                last.then_inc(group_done, 1)
            pe.wait_ge(s_rows, 16 * 9)
            pe.wait_ge(s_rb, 16)
            g = flat(claim("cols", "dve"))
            pe.transpose(g[:, 0:N_BIAS], brows[0:N_BIAS, :], ident[0:N_BIAS, 0:N_BIAS])
            pe.transpose(g[:, N_BIAS:N_BIAS + N_GAIN], grows[0:N_GAIN, :], ident[0:N_GAIN, 0:N_GAIN])
            mm(g[:, 512:512 + NE], ones[0:1, :], rbrow[0:1, :]).then_inc(group_done, 1)
            pe.wait_ge(csilu_ready, 1)
            g = flat(claim("cs", "act"))
            for t in range(DT):
                last = pe.transpose(g[:, t * NSEQ:(t + 1) * NSEQ], csilu[0:NSEQ, t * P:(t + 1) * P],
                                    ident[0:NSEQ, 0:NSEQ])
            last.then_inc(group_done, 1)
            norm_sum(0)
            taken("cs")
            pe.wait_ge(cs_zeroed, 1)
            fill(4)
            turn_up_to(4)

            wait_h(0)

            def w_heads(h, a, b):
                cut = lambda part: ktile(A["ret_w_in"][0][:, part * D + h * RD:part * D + (h + 1) * RD])
                return [(lambda w: w3(w, DT, 512)[:, :, 0:RD], cut(a)),
                        (lambda w: w3(w, DT, 512)[:, :, RD:512], cut(b))]

            def project_qk(h):
                w = w3(load(("qk", h), w_heads(h, 0, 1)), DT, 512)
                for j, n in enumerate("qk"):
                    for t in range(2):
                        c = j * RD + t * P
                        project((n, h, t), "dve", [w[:, k, c:c + P] for k in range(DT)], h_all)
                used(("qk", h))

            project_qk(0)
            pe.wait_ge(s_tab2, 16)
            for h in range(RH):
                w = w3(load(("vg", h), w_heads(h, 2, 3)), DT, 512)
                g = flat(claim(("v", h), "act"))
                for i in range(4):
                    for k in range(DT):
                        last = mm(g[:, i * RD:(i + 1) * RD], h_tile(k, i), w[:, k, 0:RD],
                                  k == 0, k == DT - 1)
                last.then_inc(group_done, 1)
                g = flat(claim(("vs", h), "act"))
                for k in range(DT):
                    last = mm(g[0:NS, 0:RD], h_tile(k, 4), w[:, k, 0:RD], k == 0, k == DT - 1)
                last.then_inc(group_done, 1)
                for t in range(2):
                    c = RD + t * P
                    project(("g", h, t), "act", [w[:, k, c:c + P] for k in range(DT)], h_all)
                used(("vg", h))
                fill()
                pe.wait_ge(k_ready, h + 1)
                g = flat(claim(("kt", h), "act"))
                for j in range(4):
                    for t in range(2):
                        last = pe.transpose(g[:, j * RD + t * P:j * RD + (t + 1) * P], kT[:, t, j * P:(j + 1) * P],
                                            ident)
                last.then_inc(group_done, 1)
                g = flat(claim(("ks", h), "dve"))
                for t in range(2):
                    last = pe.transpose(g[0:NS, t * P:(t + 1) * P], kT[:, t, NP:T], ident)
                last.then_inc(group_done, 1)
                pe.wait_ge(q_ready, h + 1)
                for pr, js in (("sa", (0, 1)), ("sb", (2, 3))):
                    g = claim((pr, h), "dve")
                    for b, j in enumerate(js):
                        for t in range(2):
                            last = mm(g[:, b, 0:NP - P * j], kT[:, t, j * P:(j + 1) * P], qT[:, t, j * P:NP],
                                      t == 0, t == 1)
                    last.then_inc(group_done, 1)
                fill()
                taken(("sb", h))
                taken(("vs", h))
                g = claim(("o", h), "dve")
                for t in range(2):
                    for j in range(4):
                        last = mm(g[:, t, j * P:NP], vtok[:, j, t * P:(t + 1) * P], PT[j], j == 0, j == 3)
                last.then_inc(group_done, 1)
                taken(("kt", h))
                g = flat(claim(("st", h), "act"))
                for t in range(2):
                    for j in range(4):
                        last = mm(g[:, t * RD:(t + 1) * RD], kdec[:, j, t * P:(t + 1) * P], vtok[:, j, :],
                                  j == 0, j == 3)
                last.then_inc(group_done, 1)
                pe.wait_ge(km_ready, h + 1)
                for b2 in range(4):
                    g = claim(("kv", h, b2), "dve")
                    for b in range(2):
                        for t in range(2):
                            last = mm(g[:, b, t * RD:(t + 1) * RD], kmask[0:NS, 2 * b2 + b, t * P:(t + 1) * P],
                                      vtok[0:NS, 4, :])
                    last.then_inc(group_done, 1)
                fill()
                S = load(("S", h), [(lambda w, t=t: states(w)[:, :, t, :], state_rows(A["state_ret"], h, t))
                                    for t in range(2)])
                S = states(S)
                pe.wait_ge(st_updated, h + 1)
                g = claim(("os", h), "act")
                for a in range(2):
                    for d in range(2):
                        for j in range(4):
                            b = 4 * a + j
                            last = mm(g[32 * j:32 * j + 32, a, 0:RD],
                                      qT[:, d, NP + b:NP + b + 1].broadcast_to([P, 32]), S[:, b, d, :],
                                      d == 0, d == 1)
                last.then_inc(group_done, 1)
                used(("S", h))
                fill()
                taken(("os", h))
                g = flat(claim(("ot", h), "dve"))
                for t in range(2):
                    for a in range(2):
                        last = pe.transpose(g[:, (2 * t + a) * P:(2 * t + a + 1) * P],
                                            osb[:, a, t * P:(t + 1) * P], ident)
                last.then_inc(group_done, 1)
                pe.wait_ge(o_ready, h + 1)
                project(("mu", h), "dve", [inv256] * 2, [two(oT[:, t, :]) for t in range(2)])
                fill()
                pe.wait_ge(osq_ready, h + 1)
                project(("var", h), "act", [ones] * 2, [two(sq[:, t, :]) for t in range(2)])
                fill()
                if h + 1 < RH:
                    project_qk(h + 1)
                w = load(("wout", h), [(lambda w: w3(w, 2, D), ktile(A["ret_w_out"][0][h * RD:(h + 1) * RD]))])
                w = w3(w, 2, D)
                pe.wait_ge(y_ready, h + 1)
                for t in range(DT):
                    project(("y", h, t), "dve", [w[:, k, t * P:(t + 1) * P] for k in range(2)],
                            [yT[:, k, :, :] for k in range(2)])
                used(("wout", h))
            fill(ADA_UNITS)

            def moe(l):
                s = L[l]
                nk = 1 + 3 * l
                norm_sum(nk)
                wait_h(nk)
                for i in range(5):
                    g = flat(claim(("ht", l, i), "act"))
                    n = P if i < 4 else NS
                    for t in range(DT):
                        if i < 4:
                            need_h(i // 2, t)
                        last = pe.transpose(g[0:n, t * P:(t + 1) * P], h_tile(t, i), ident)
                    last.then_inc(group_done, 1)
                if l == 0:
                    pe.wait_ge(s_rw, 16)
                g = claim(("rt", l), "act")
                for k in range(DT):
                    j = k % 4
                    for a in range(2):
                        last = mm(g[32 * j:32 * j + 32, a, 0:HALF], rw[:, k, :], hT[:, k, a, :], k < 4, k >= 4)
                last.then_inc(group_done, 1)
                w1 = w3(load(("wsg", l), [(lambda w: w3(w, DT, FE), ktile(A["shared_w_gate"][l]))]), DT, FE)
                w2 = w3(load(("wsu", l), [(lambda w: w3(w, DT, FE), ktile(A["shared_w_up"][l]))]), DT, FE)
                for f in range(FT):
                    project(("sg", l, f), "act", [w1[:, k, f * P:(f + 1) * P] for k in range(DT)], h_all)
                    if f == 0:
                        taken(("rt", l))
                        g = flat(claim(("ru", l), "dve"))
                        for i in range(5):
                            n = P if i < 4 else NS
                            src = lg[:, i // 2, (i % 2) * P:(i % 2) * P + P] if i < 4 else lgs
                            last = pe.transpose(g[0:n, i * P:(i + 1) * P], src, ident)
                        last.then_inc(group_done, 1)
                    if f == 1:
                        pe.wait_ge(s["mask_ready"], 1)
                        g = flat(claim(("cnt", l), "dve"))
                        M = R["M"].rearrange("p a b -> p (a b)")
                        mm(g[:, 0:5 * NE], tri, M)
                        mm(g[:, 512:512 + 5 * NE], ones, M).then_inc(group_done, 1)
                    if f == 3:
                        pe.wait_ge(s["tab_in"], 16)
                        g = flat(claim(("ix", l), "dve"))
                        pe.transpose(g[:, 0:TABLE], tabr[0:TABLE, :], ident[0:TABLE, 0:TABLE]).then_inc(group_done, 1)
                    project(("su", l, f), "dve", [w2[:, k, f * P:(f + 1) * P] for k in range(DT)], h_all)
                used(("wsg", l))
                used(("wsu", l))

                base = len(loads) % 6
                s["base"] = base
                s["prior"] = len(loads)
                for w_, c_ in group_who[-4:]:
                    pe.wait_ge(took[w_], c_)
                psH = PS[:, 0:2, :].rearrange("p a b -> p (a b)")
                psG, psU = PS[:, 2, :], PS[:, 3, :]
                psX = PS[:, 4, :]
                psY = PS[:, 5:7, :]
                wg = [W[:, (base + 3 * u) % 6, :].rearrange("p (t n) -> p t n", t=DT) for u in range(2)]
                wu = [W[:, (base + 3 * u + 1) % 6, :].rearrange("p (t n) -> p t n", t=DT) for u in range(2)]
                wd = [W[:, (base + 3 * u + 2) % 6, :].rearrange("p (t n) -> p t n", t=FT) for u in range(2)]

                def turn_h(u):
                    for t in range(DT):
                        last = pe.transpose(psH[:, t * P:(t + 1) * P], hblk[u][:, t * P:(t + 1) * P], ident)
                    last.then_inc(s["th_done"], 1)

                def up_or_gate(out, u, w, ks):
                    for k in ks:
                        last = mm(out, hbT[u][:, k, :], w[:, k, :], k == 0, k == DT - 1)
                    return last

                def block_of(b, u, nth, land, first=False, last_block=False):
                    if not last_block:
                        pe.wait_ge(s["gathered"][1 - u], land)
                        turn_h(1 - u)
                    pe.wait_ge(s["w_in"][3 * u + 1], nth * 16 + 16)
                    if not first:
                        pe.wait_ge(s["hid_ready"], b)
                    up_or_gate(psU, u, wu[u], range(DT)).then_inc(s["w_used"], 1)
                    if not last_block:
                        pe.wait_ge(s["w_in"][3 * (1 - u)], land)
                        pe.wait_ge(s["hb_ready"], b + 2)
                        pe.wait_ge(s["sg_ready"], b + 1)
                        up_or_gate(psG, 1 - u, wg[1 - u], range(DT // 2))
                    pe.wait_ge(s["hid_ready"], b + 1)
                    if not first:
                        pe.wait_ge(s["hidT_ready"], b)
                    for f in range(FT):
                        last = pe.transpose(psX[:, f * P:(f + 1) * P], hid[:, f * P:(f + 1) * P], ident)
                    last.then_inc(s["ht_done"], 1)
                    if not last_block:
                        up_or_gate(psG, 1 - u, wg[1 - u], range(DT // 2, DT)).then_inc(s["w_used"], 1)
                    pe.wait_ge(s["w_in"][3 * u + 2], nth * 16 + 16)
                    pe.wait_ge(s["hidT_ready"], b + 1)
                    if not first:
                        pe.wait_ge(s["yout_ready"], b)
                    for n in range(2):
                        for f in range(FT):
                            last = mm(psY[:, n, :], hidT[:, f, :], wd[u][:, f, n * 512:(n + 1) * 512],
                                      f == 0, f == FT - 1)
                    last.then_inc(s["w_used"], 1)

                pe.sem_inc(s["w_used"], 1)
                pe.wait_ge(s["gathered"][0], 16)
                turn_h(0)
                pe.wait_ge(s["w_in"][0], 16)
                pe.wait_ge(s["hb_ready"], 1)
                up_or_gate(psG, 0, wg[0], range(DT)).then_inc(s["w_used"], 1)
                block_of(0, 0, 0, 16, first=True)
                pe.wait_ge(s["route_ready"], 1)
                turns = pe.value_load(niter[0:1, 0:1], min_val=NE // 2 - 1, max_val=MAXBLK // 2 - 1)
                with pe.Fori(0, turns) as it:
                    block_of(it * 2 + 1, 1, it, it * 16 + 32)
                    block_of(it * 2 + 2, 0, it + 1, it * 16 + 32)
                block_of(turns * 2 + 1, 1, turns, None, last_block=True)
                pe.wait_ge(s["yout_ready"], turns * 2 + 2)
                w = w3(load(("wsd", l), [(lambda w: w3(w, FT, D), ktile(A["shared_w_down"][l]))]), FT, D)
                pe.wait_ge(s["shT_ready"], FT)
                for t in range(DT):
                    project(("sd", l, t), "dve", [w[:, k, t * P:(t + 1) * P] for k in range(FT)],
                            [shT[:, k, :, :] for k in range(FT)])
                used(("wsd", l))
                for i in range(5):
                    pe.wait_ge(s["comb_ready"], i + 1)
                    g = flat(claim(("cb", l, i), "dve"))
                    n = P if i < 4 else NS
                    for t in range(DT):
                        last = pe.transpose(g[:, t * P:t * P + n],
                                            hbT[i % 2].rearrange("p t n -> p (t n)")[0:n, t * P:(t + 1) * P],
                                            ident[0:n, 0:n])
                    last.then_inc(group_done, 1)

            moe(0)

            norm_sum(2)
            wait_h(2)
            w = w3(load("dkv", [(lambda w: w3(w, DT, LAT + ROPE), ktile(A["mla_w_dkv"]))]), DT, LAT + ROPE)
            for t in range(2):
                project(("z", t), "act", [w[:, k, t * P:(t + 1) * P] for k in range(DT)], h_all)
            project("zk", "act", [w[:, k, LAT:LAT + ROPE] for k in range(DT)], h_all, ROPE)
            used("dkv")
            taken("zk")
            project("kr", "dve", [cst("rot")[0:ROPE, :]], [zk[0:ROPE, :, :]], ROPE)
            pe.wait_ge(msq_ready, 1)
            project("zss", "act", [ones] * 2, [msq[:, t, :, :] for t in range(2)])
            wait_h(3)
            w = w3(load("dq", [(lambda w: w3(w, DT, LAT), ktile(A["mla_w_dq"][0]))]), DT, LAT)
            for t in range(2):
                project(("cq", t), "act", [w[:, k, t * P:(t + 1) * P] for k in range(DT)], h_all)
            used("dq")
            pe.wait_ge(ckv_ready, 1)
            pe.wait_ge(kpe_ready, 1)
            for i0 in (0, 2, 4):
                g = claim(("ct", i0), "act")
                for i in range(i0, min(i0 + 2, 5)):
                    n = P if i < 4 else NS
                    for t in range(2):
                        pe.transpose(g[0:n, i - i0, t * P:(t + 1) * P], ckvT[:, t, i * P:i * P + n], ident)
                    last = pe.transpose(g[0:n, i - i0, LAT:LAT + ROPE], kpeT[0:ROPE, i * P:i * P + n],
                                        ident[0:ROPE, 0:ROPE])
                last.then_inc(group_done, 1)
            pe.wait_ge(msq_ready, 2)
            project("qss", "act", [ones] * 2, [msq[:, t, :, :] for t in range(2)])
            w = w3(load("uv", [(lambda w: w3(w, MH, LAT), A["mla_w_uv"].rearrange("h v c -> v h c"))]), MH, LAT)
            for half in range(2):
                g = flat(claim(("uv", half), "act"))
                for j in range(8):
                    h, t = half * 4 + j // 2, j % 2
                    last = pe.transpose(g[:, j * P:(j + 1) * P], w[:, h, t * P:(t + 1) * P], ident)
                last.then_inc(group_done, 1)
            used("uv")
            pe.wait_ge(cq_ready, 1)
            QW = NOPE + ROPE
            wq = w3(load("uq", [(lambda w: w3(w, 2, MH * QW), ktile(A["mla_w_uq"][0]))]), 2, MH * QW)
            wk = w3(load("uk", [(lambda w: w3(w, MH, LAT), A["mla_w_uk"].rearrange("h n c -> n h c"))]), MH, LAT)
            cq_all = [cqT[:, k, :, :] for k in range(2)]
            def query_cols(h):
                project(("qn", h), "act", [wq[:, k, h * QW:h * QW + NOPE] for k in range(2)], cq_all)
                project(("qp", h), "act", [wq[:, k, h * QW + NOPE:(h + 1) * QW] for k in range(2)], cq_all, ROPE)
                taken(("qn", h))
                for t in range(2):
                    project(("ql", h, t), "dve", [wk[:, h, t * P:(t + 1) * P]], [qn])

            def query_rotary(h):
                taken(("qp", h))
                project(("qr", h), "dve", [cst("rot")[0:ROPE, :]], [qpr[0:ROPE, :, :]], ROPE)

            def values(h):
                taken(("ol", h))
                g = claim(("ov", h), "act")
                for t in range(2):
                    last = mm(g[:, 0, :], uvT[:, h, t, :], olat[:, t, :], t == 0, t == 1)
                last.then_inc(group_done, 1)

            query_cols(0)
            query_rotary(0)
            for h in range(MH):
                pe.wait_ge(ql_ready, h + 1)
                pe.wait_ge(qpe_ready, h + 1)
                for name, chunks in SCORES:
                    g = flat(claim((name, h), "act"))
                    for i, at in chunks:
                        o = g[:, at:at + (i + 1) * P]
                        for t in range(2):
                            mm(o, ql[:, t, i * P:(i + 1) * P], ckvT[:, t, 0:(i + 1) * P], t == 0, False)
                        last = mm(o, qpe[0:ROPE, i * P:(i + 1) * P], kpeT[0:ROPE, 0:(i + 1) * P], False, True)
                    last.then_inc(group_done, 1)
                if h:
                    values(h - 1)
                if h + 1 < MH:
                    query_cols(h + 1)
                pe.wait_ge(p_ready, h + 1)
                for name, chunks in TURNS:
                    g = flat(claim((name, h), "act"))
                    for i, at in chunks:
                        for j in range(i + 1):
                            last = pe.transpose(g[:, at + j * P:at + (j + 1) * P], pr_[:, TRI[i] + j * P:TRI[i] + (j + 1) * P],
                                                ident)
                    last.then_inc(group_done, 1)
                if h + 1 < MH:
                    query_rotary(h + 1)
                taken(("ptb", h))
                g = claim(("ol", h), "dve")
                for t in range(2):
                    for j in range(4):
                        last = mm(g[:, t, j * P:NP], ctok[:, j, t * P:(t + 1) * P], PTm[:, j, j * P:NP],
                                  j == 0, j == 3)
                last.then_inc(group_done, 1)
            values(MH - 1)
            used("uq")
            used("uk")
            pages, PW = {}, LAT + ROPE

            def scan(b):
                if b == TAIL_SEQ:
                    pages[b] = [W[:, load_no[("pages", h)] % 6, NPAGE * PW + pg * PW:NPAGE * PW + (pg + 1) * PW]
                                for h in TAILS for pg in range(TAIL_PAGES)]
                else:
                    w = load(("pages", b), None)
                    pages[b] = [w[:, pg * PW:(pg + 1) * PW] for pg in range(NPAGE)]
                pe.wait_ge(kpe_in[b], 16 * NPAGE)
                for t in range(3):
                    g = flat(claim(("kt3", b, t), "act" if t % 2 else "dve"))
                    m = P if t < 2 else ROPE
                    for pg in range(NPAGE):
                        last = pe.transpose(g[0:m, pg * P:(pg + 1) * P], pages[b][pg][:, t * P:t * P + m], ident)
                    last.then_inc(group_done, 1)
                g = flat(claim(("sp", b), "dve"))
                for t in range(3):
                    taken(("kt3", b, t))
                    m = P if t < 2 else ROPE
                    for c in range(4):
                        last = mm(g[32 * c:32 * c + 32, 0:256], qsl[0:m, t, b, :],
                                  KT[0:m, t, c * 256:(c + 1) * 256], t == 0, t == 2)
                last.then_inc(group_done, 1)

            def scan_new(q):
                pe.wait_ge(prodn_ready, q + 1)
                g = flat(claim(("sn", q), "dve"))
                for t in range(3):
                    m = P if t < 2 else ROPE
                    last = mm(g[:, 0:1], prodn[0:m, t, :], ones[0:m, 0:1], t == 0, t == 2)
                last.then_inc(group_done, 1)

            def attend(q):
                pe.wait_ge(sp_ready, q + 1)
                g = flat(claim(("pts", q), "act"))
                for pg in range(NPAGE):
                    last = pe.transpose(g[:, pg * P:(pg + 1) * P], Ps[:, pg * P:(pg + 1) * P], ident)
                last.then_inc(group_done, 1)
                taken(("pts", q))
                g = claim(("pv", q), "dve")
                mm(g[:, 1, 0:LAT], cst("selq")[0:NS, q * P:(q + 1) * P], ctok[0:NS, 4, 0:LAT])
                for pg in range(NPAGE):
                    for j in range(4):
                        last = mm(g[32 * j:32 * j + 32, 0, 0:LAT], PTs[:, pg, 32 * j:32 * j + 32],
                                  pages[4 * q + j][pg][:, 0:LAT], pg == 0, pg == NPAGE - 1)
                last.then_inc(group_done, 1)
                for b in ((0, 1), (2, 3, 4, 5, 7))[q]:
                    used(("pages", b))
                pe.wait_ge(olr_ready, q + 1)
                g = flat(claim(("olt", q), "dve"))
                for t in range(2):
                    last = pe.transpose(g[:, t * P:(t + 1) * P], olr[:, t * P:(t + 1) * P], ident)
                last.then_inc(group_done, 1)

            for b in range(4):
                scan(b)
            scan_new(0)
            scan(4)
            attend(0)
            for b in range(5, NS):
                scan(b)
            scan_new(1)
            attend(1)
            taken(("olt", 1))
            g = flat(claim("ovs", "act"))
            for h in range(MH):
                for t in range(2):
                    last = mm(g[:, h * NS:(h + 1) * NS], uvT[:, h, t, :], osl[:, t, :, h], t == 0, t == 1)
            last.then_inc(group_done, 1)
            taken(("ov", MH - 1))
            taken("ovs")
            for c in range(2):
                w = w3(load(("wo", c), [(lambda w: w3(w, DT, 512), ktile(A["mla_w_o"][0][:, c * 512:(c + 1) * 512]))]),
                       DT, 512)
                for t in range(4):
                    project(("mo", 4 * c + t), "dve", [w[:, k, t * P:(t + 1) * P] for k in range(DT)], h_all)
                used(("wo", c))

            moe(1)

            norm_sum(5)
            pe.wait_ge(hs_ready, 6)
            for i in range(5):
                g = flat(claim(("out", i), "act"))
                n = P if i < 4 else NS
                for t in range(DT):
                    if i in (0, 2):
                        pe.wait_ge(h_scaled, (2 * 5 + i // 2) * DT + t + 1)
                    last = pe.transpose(g[0:n, t * P:(t + 1) * P], h_tile(t, i), ident)
                last.then_inc(group_done, 1)

        seen = {"dve": 0, "act": 0}

        def group(eng, who, name):
            n = group_no[name]
            seen[who] += 1
            assert group_who[n] == (who, seen[who]), (name, group_who[n], seen[who])
            eng.wait_ge(group_done, n + 1)
            return pair(n)

        @block.scalar
        def _(act):
            chain = [0]
            act_chain = sem("act_chain")

            def link(ins):
                chain[0] += 1
                ins.then_inc(act_chain, 1)
                act.wait_ge(act_chain, chain[0])

            def grp(name):
                return group(act, "act", name)

            freed = took["act"]
            cp = lambda o, i, **k: act.activation(o, i, ACT.Copy, **k)

            act.dma_start(C[:, 0:FIRST], A["tables"][:, 0:FIRST]).then_inc(s_tab, 16)
            act.dma_start(crow[0:1, :], A["c_prompt"]).then_inc(s_c, 16)
            act.dma_start(crow[1:NSEQ, :], A["c_sample"]).then_inc(s_c, 16)
            rows = lambda a: a.rearrange("(t p) -> t p", p=P)
            act.dma_start(brows[0:96, :], A["b_ada"].rearrange("l (t p) -> (l t) p", p=P)).then_inc(s_rows, 16)
            act.dma_start(brows[96:112, :], rows(A["kv_b_ada"])).then_inc(s_rows, 16)
            act.dma_start(grows[G_MIX:G_FFN, :], A["norm_mix_g"].rearrange("l (t p) -> (l t) p", p=P)).then_inc(s_rows, 16)
            act.dma_start(grows[G_FFN:G_KV, :], A["norm_ffn_g"].rearrange("l (t p) -> (l t) p", p=P)).then_inc(s_rows, 16)
            act.dma_start(grows[G_KV:G_GN, :], rows(A["kv_norm_g"])).then_inc(s_rows, 16)
            act.dma_start(grows[G_GN:G_FIN, :], A["ret_gn_g"].rearrange("l (t p) -> (l t) p", p=P)).then_inc(s_rows, 16)
            act.dma_start(grows[G_FIN:G_CKV, :], rows(A["final_norm_g"])).then_inc(s_rows, 16)
            act.dma_start(grows[G_CKV:G_CQ, :], rows(A["mla_kv_norm_g"])).then_inc(s_rows, 16)
            act.dma_start(grows[G_CQ:N_GAIN, :], A["mla_q_norm_g"].rearrange("l (t p) -> (l t) p", p=P)).then_inc(s_rows, 16)
            act.wait_ge(s_c, 32)
            act.activation(csilu[0:NSEQ, :], crow[0:NSEQ, :], ACT.Silu).then_inc(csilu_ready, 1)
            g = flat(grp("cs"))
            act.wait_ge(cs_zeroed, 1)
            cp(csT[:, :, 0:NSEQ], g[:, 0:DT * NSEQ].rearrange("p (a b) -> p a b", a=DT)).then_inc(freed, 1)
            ada_next = [0]

            def fill(n=1):
                for _ in range(n):
                    u = ada_next[0]
                    ada_next[0] += 1
                    if u < ADA_UNITS:
                        g = flat(grp(("ada", u)))
                        cp(apart[:, u % 2, 0:512], g[:, 0:512]).then_inc(freed, 1)

            def norm(k, x_need, shift, same_x=False, between=None):
                if not same_x:
                    act.wait_ge(x_updated, x_need)
                    for t in range(DT):
                        act.activation(hT[:, t, :, :], xT[:, t, :, :], ACT.Square,
                                       scale=D ** -0.5).then_inc(sq_ready, 1)
                    g = grp(("ss", k))
                    act.activation(rs[:, :, :], xw(g), ACT.Sqrt, bias=cst("eps")).then_inc(freed, 1)
                if between is not None:
                    between()
                if shift is not None:
                    for a in range(2):
                        for t in range(DT):
                            act.wait_ge(h_scaled, (2 * k + a) * DT + t + 1)
                            act.activation(hT[:, t, a, 0:HP], hT[:, t, a, 0:HP], ACT.Identity,
                                           bias=mod[:, shift + t, 0:1]).then_inc(h_ready, 1)

            norm(0, 5, 0, between=lambda: fill(4))
            act.wait_ge(s_tab2, 16)
            for h in range(RH):
                g = flat(grp(("v", h)))
                cp(vtok[:, 0:4, :].rearrange("p a b -> p (a b)"), g).then_inc(freed, 1)
                g = flat(grp(("vs", h)))
                act.activation(vtok[0:NS, 4, :], g[0:NS, 0:RD], ACT.Copy).then_inc(freed, 1)
                for t in range(2):
                    g = grp(("g", h, t))
                    act.activation(gT[:, t, :, :], xw(g), ACT.Silu).then_inc(freed, 1)
                fill()
                g = flat(grp(("kt", h)))
                for j in range(4):
                    s0 = AT["kdec"][0] + 4 * h + j
                    last = cp(kdec[:, j, :], g[:, j * RD:(j + 1) * RD], scale=C[:, s0:s0 + 1])
                last.then_inc(freed, 1)
                fill()
                g = flat(grp(("st", h)))
                if h:
                    act.wait_ge(st_out, 16 * h)
                else:
                    act.wait_ge(z_out, 16 * 2 * (MAXBLK - NE))
                cp(stout.rearrange("p a b -> p (a b)"), g[:, 0:2 * RD]).then_inc(freed, 1)
                act.wait_ge(freed, seen["act"])
                act.dma_start(O["state_p"][0, 0, h].rearrange("(t p) v -> p t v", p=P), stout).then_inc(st_out, 16)
                act.wait_ge(st_updated, h + 1)
                slot = load_no[("S", h)] % 6
                for t in range(2):
                    act.dma_start(state_rows(O["state_s"], h, t),
                                  states(W[:, slot, :])[:, :, t, :]).then_inc(ss_out[h], 16)
                fill()
                g = grp(("os", h))
                cp(osb, g[:, :, 0:RD]).then_inc(freed, 1)
                fill()
                act.wait_ge(oc_ready, h + 1)
                act.activation(sq.rearrange("p a b -> p (a b)"), oT.rearrange("p a b -> p (a b)"), ACT.Square,
                               scale=RD ** -0.5).then_inc(osq_ready, 1)
                fill()
                g = grp(("var", h))
                act.activation(rs2, xw(g), ACT.Sqrt, bias=cst("eps")).then_inc(freed, 1)
                fill()
            fill(ADA_UNITS)

            def moe(l, x_need):
                s = L[l]
                norm(1 + 3 * l, x_need, 48 * l + 24)
                for i in range(5):
                    g = flat(grp(("ht", l, i)))
                    n = P if i < 4 else NS
                    if i >= 2:
                        act.wait_ge(s["rows_out"][i % 2], 16 * (i // 2))
                    cp(ysb[i % 2][0:n, :], g[0:n, :]).then_inc(freed, 1)
                    act.wait_ge(freed, seen["act"])
                    act.dma_start(h_dram[l][i * P:i * P + n, :], ysb[i % 2][0:n, :]).then_inc(s["rows_out"][i % 2], 16)
                g = grp(("rt", l))
                cp(lgs.rearrange("p (a b) -> p a b", a=2), g[:, :, HP:HALF])
                cp(lg, xw(g)).then_inc(freed, 1)
                for f in range(FT):
                    g = grp(("sg", l, f))
                    if f:
                        act.wait_ge(s["shT_ready"], f)
                    act.activation(sgs, xw(g), ACT.Silu).then_inc(freed, 1)
                    if f == 0:
                        act.wait_ge(s["logits_ready"], 1)
                        act.activation(R["sc"][:, 0:4, :], R["sc"][:, 0:4, :], ACT.Sigmoid)
                        act.activation(R["sc"][0:NS, 4, :], R["sc"][0:NS, 4, :], ACT.Sigmoid).then_inc(s["scores_ready"], 1)
                psH = PS[:, 0:2, :].rearrange("p a b -> p (a b)")

                psY = PS[:, 5:7, :].rearrange("p a b -> p (a b)")

                def copy_h(u, need):
                    act.wait_ge(s["th_done"], need)
                    cp(hbT[u].rearrange("p t n -> p (t n)"), psH).then_inc(s["hb_ready"], 1)

                def y_rows(u, nth, used):
                    act.wait_ge(s["w_used"], used)
                    if nth is not None:
                        act.wait_ge(s["stored"][u], nth * 16)
                    cp(ysb[u], psY).then_inc(s["yout_ready"], 1)

                def block_of(b, u, before, first=False, last_block=False):
                    act.wait_ge(s["w_used"], 2 if first else b * 3 + 1)
                    if not first:
                        act.wait_ge(s["hid_ready"], b)
                    act.activation(sg, PS[:, 2, :], ACT.Silu).then_inc(s["sg_ready"], 1)
                    if not first:
                        y_rows(1 - u, before, b * 3 + 2)
                    if not last_block:
                        copy_h(1 - u, b + 2)

                act.wait_ge(s["rows_out"][0], 48)
                act.wait_ge(s["rows_out"][1], 32)
                copy_h(0, 1)
                block_of(0, 0, None, first=True)
                block_of(1, 1, None)
                block_of(2, 0, None)
                act.wait_ge(s["route_ready"], 1)
                turns = act.value_load(niter[0:1, 0:1], min_val=NE // 2 - 1, max_val=MAXBLK // 2 - 1)
                with act.Fori(1, turns) as it:
                    block_of(it * 2 + 1, 1, it)
                    block_of(it * 2 + 2, 0, it)
                block_of(turns * 2 + 1, 1, turns, last_block=True)
                y_rows(1, turns, turns * 6 + 7)
                for i in range(5):
                    n = P if i < 4 else NS
                    act.wait_ge(s["got"][2 * i], 16)
                    if i >= 2:
                        act.wait_ge(group_done, group_no[("cb", l, i - 2)] + 1)
                    act.activation(hbT[i % 2].rearrange("p t n -> p (t n)")[0:n, :], y_pair(l, i)[0][0:n, :], ACT.Copy,
                                   scale=R5["w1"][0:n, i:i + 1]).then_inc(s["first_weighted"], 1)

            moe(0, 5 + DT * RH)
            XN = 5 + DT * RH + DT + 5
            norm(2, XN, 96)
            for t in range(2):
                g = grp(("z", t))
                cp(zT[:, t, :, :], xw(g)).then_inc(freed, 1)
            g = grp("zk")
            cp(zk[0:ROPE, :, :], xw(g)[0:ROPE]).then_inc(freed, 1)
            act.wait_ge(freed, seen["act"])
            for t in range(2):
                last = act.activation(msq[:, t, :, :], zT[:, t, :, :], ACT.Square, scale=LAT ** -0.5)
            last.then_inc(msq_ready, 1)
            g = grp("zss")
            act.activation(rl, xw(g), ACT.Sqrt, bias=cst("eps")).then_inc(freed, 1)
            norm(3, XN, 48, same_x=True)
            act.wait_ge(ckv_ready, 1)
            for t in range(2):
                g = grp(("cq", t))
                cp(zT[:, t, :, :], xw(g)).then_inc(freed, 1)
            act.wait_ge(freed, seen["act"])
            for t in range(2):
                last = act.activation(msq[:, t, :, :], zT[:, t, :, :], ACT.Square, scale=LAT ** -0.5)
            last.then_inc(msq_ready, 1)
            for i0 in (0, 2, 4):
                g = grp(("ct", i0))
                if i0 < 4:
                    cp(ctok[:, i0:i0 + 2, :], g[:, :, 0:LAT + ROPE]).then_inc(freed, 1)
                else:
                    cp(ctok[0:NS, 4, :], g[0:NS, 0, 0:LAT + ROPE]).then_inc(freed, 1)
            act.wait_ge(freed, seen["act"])
            act.dma_start(O["ckv_p"][0].rearrange("(i p) c -> p i c", p=P), ctok[:, 0:4, 0:LAT]).then_inc(outs_done, 16)
            act.dma_start(O["kpe_p"][0].rearrange("(i p) c -> p i c", p=P), ctok[:, 0:4, LAT:]).then_inc(outs_done, 16)
            act.dma_start(O["ckv_s"].rearrange("b a c -> (b a) c"), ctok[0:NS, 4, 0:LAT]).then_inc(outs_done, 16)
            act.dma_start(O["kpe_s"].rearrange("b a c -> (b a) c"), ctok[0:NS, 4, LAT:]).then_inc(outs_done, 16)
            g = grp("qss")
            act.activation(rl, xw(g), ACT.Sqrt, bias=cst("eps")).then_inc(freed, 1)
            for half in range(2):
                g = flat(grp(("uv", half)))
                cp(uvT[:, 4 * half:4 * half + 4, :, :].rearrange("p a b c -> p (a b c)"), g).then_inc(freed, 1)

            def query(h):
                g = grp(("qn", h))
                cp(qn, xw(g)).then_inc(freed, 1)
                g = grp(("qp", h))
                if h:
                    act.wait_ge(qpe_ready, h)
                cp(qpr[0:ROPE, :, :], xw(g)[0:ROPE]).then_inc(freed, 1)

            def values(h):
                g = grp(("ov", h))
                cp(hT[:, h, :, 0:HP], g[:, 0, :].rearrange("p (a b) -> p a b", a=2)).then_inc(freed, 1)

            query(0)
            for h in range(MH):
                act.wait_ge(mx_ready, h + 1)
                for name, chunks in SCORES:
                    g = flat(grp((name, h)))
                    for i, at in chunks:
                        last = act.activation(pr_[:, TRI[i]:TRI[i + 1]], g[:, at:at + (i + 1) * P], ACT.Exp,
                                              scale=MLA_SCALE, bias=mcol[:, 4 + i:5 + i],
                                              accum_out=mcol[:, 8 + i:9 + i])
                    last.then_inc(freed, 1)
                if h:
                    values(h - 1)
                if h + 1 < MH:
                    query(h + 1)
                for name, chunks in TURNS:
                    g = flat(grp((name, h)))
                    for i, at in chunks:
                        last = cp(PTm[:, 0:i + 1, i * P:(i + 1) * P],
                                  g[:, at:at + (i + 1) * P].rearrange("p (a b) -> p a b", a=i + 1))
                    last.then_inc(freed, 1)
            values(MH - 1)
            def scan(b):
                g = flat(grp(("kt3", b, 1)))
                cp(KT[:, 1, :], g).then_inc(freed, 1)

            def softmax(q):
                act.wait_ge(smx_ready, q + 1)
                act.activation(Ps, S_sb[q], ACT.Exp, scale=MLA_SCALE, bias=mcol2[:, 1:2],
                               accum_out=mcol2[:, 2:3]).then_inc(se_ready, 1)

            def attend(q):
                g = flat(grp(("pts", q)))
                cp(PTs.rearrange("p a b -> p (a b)"), g).then_inc(freed, 1)

            for b in range(4):
                scan(b)
            softmax(0)
            scan(4)
            attend(0)
            for b in range(5, NS):
                scan(b)
            softmax(1)
            attend(1)
            g = flat(grp("ovs"))
            cp(hT[:, :, :, HP:HALF], g[:, 0:MH * NS].rearrange("p (h a b) -> p h a b", h=MH, a=2)).then_inc(freed, 1)
            act.wait_ge(outs_done, 64)
            moe(1, XN + DT)
            norm(5, XN + DT + DT + 5, None)
            for i in range(5):
                g = flat(grp(("out", i)))
                n = P if i < 4 else NS
                if i >= 2:
                    act.wait_ge(orow_out[i % 2], 16 * (i // 2))
                cp(orow[i % 2][0:n, :], g[0:n, :]).then_inc(freed, 1)
                act.wait_ge(freed, seen["act"])
                dst = O["y_p"][0][i * P:(i + 1) * P, :] if i < 4 else O["y_s"].rearrange("b a c -> (b a) c")
                act.dma_start(dst, orow[i % 2][0:n, :]).then_inc(orow_out[i % 2], 16)
            act.wait_ge(orow_out[0], 48)
            act.wait_ge(orow_out[1], 32)
            act.wait_ge(st_out, 16 * RH)
            for h in range(RH):
                act.wait_ge(ss_out[h], 32)

        @block.vector
        def _(dve):
            chain = [0]

            def link(ins):
                chain[0] += 1
                ins.then_inc(dve_chain, 1)
                dve.wait_ge(dve_chain, chain[0])

            def settled(own):
                dve.wait_ge(took["dve"], seen["dve"])

            def grp(name):
                return group(dve, "dve", name)

            def act_took(name):
                w, c = group_who[group_no[name]]
                assert w == "act"
                dve.wait_ge(took[w], c)

            freed = took["dve"]
            tt, ts, stt = dve.tensor_tensor, dve.tensor_scalar, dve.scalar_tensor_tensor
            wide = lambda a, shape: a.broadcast_to(shape)

            ada_next, ada_turned = [0], [0]

            def turn_up_to(n):
                for u in range(ada_turned[0], n):
                    ada_turned[0] = u + 1
                    g = flat(grp(("at", u)))
                    part = g[:, 0:512].rearrange("p (c j r) -> p c r j", c=4, j=4)[:, :, 0:NSEQ, :]
                    out = asum[:, u % 2, :].rearrange("p (a b) -> p a b", a=4)
                    if u >= 2:
                        dve.wait_ge(ada_ready, u - 1)
                    dve.tensor_reduce(out, part, AX.X, ALU.add).then_inc(freed, 1)
                    settled("asum")
                    tt(mod[:, 4 * u:4 * u + 4, :], out,
                       wide(cols[:, 4 * u:4 * u + 4].unsqueeze(2), [P, 4, NSEQ]), ALU.add).then_inc(ada_ready, 1)

            def fill(n=1):
                for _ in range(n):
                    turn_up_to(min(ada_next[0], ADA_UNITS))
                    ada_next[0] += 1

            def mods_ready(j):
                dve.wait_ge(ada_ready, j // 4 + 1)

            def norm(k, shift, gain, modulated=True, same_x=False):
                g8 = cols[:, N_BIAS + gain:N_BIAS + gain + DT]
                if modulated:
                    mods_ready(shift + 15)
                    link(stt(acol[:, :, :], mod[:, shift + 8:shift + 16, :], 1.0,
                             wide(g8.unsqueeze(2), [P, DT, NSEQ]), ALU.add, ALU.mult))
                if not same_x:
                    act_took(("ss", k))
                    link(dve.reciprocal(rs[:, :, HP:HALF], rs[:, :, HP:HALF]))
                hs, xs = hT[:, :, :, HP:HALF], xT[:, :, :, HP:HALF]
                link(tt(hs, xs, wide(rs[:, :, HP:HALF].unsqueeze(1), [P, DT, 2, HS]), ALU.mult))
                if modulated:
                    link(tt(hs, hs, acol[:, :, 1:NSEQ].rearrange("p t (a b) -> p t a b", a=2), ALU.mult))
                    link(tt(hs, hs, mod[:, shift:shift + DT, 1:NSEQ].rearrange("p t (a b) -> p t a b", a=2),
                            ALU.add))
                else:
                    link(tt(hs, hs, wide(g8.unsqueeze(2), [P, DT, NS]).rearrange("p t (a b) -> p t a b", a=2),
                            ALU.mult))
                dve.tensor_copy(hS[:, :, :].rearrange("p t (a b) -> p t a b", a=2), hs).then_inc(hs_ready, 1)
                for a in range(2):
                    if not same_x:
                        link(dve.reciprocal(rs[:, a, 0:HP], rs[:, a, 0:HP]))
                    for t in range(DT):
                        scale = acol[:, t, 0:1] if modulated else g8[:, t:t + 1]
                        stt(hT[:, t, a, 0:HP], xT[:, t, a, 0:HP], scale, rs[:, a, 0:HP],
                            ALU.mult, ALU.mult).then_inc(h_scaled, 1)

            xup = [5]

            def residual(name, t, gate):
                g = grp(name)
                if t == 0:
                    mods_ready(gate + 7)
                    dve.wait_ge(x_updated, xup[0])
                link(tt(tmp8[:, t, :, :], xw(g)[:, :, HP:HALF], smp(mod[:, gate + t, 1:NSEQ]), ALU.mult))
                stt(xT[:, t, :, 0:HP], g[:, :, 0:HP], mod[:, gate + t, 0:1], xT[:, t, :, 0:HP],
                    ALU.mult, ALU.add).then_inc(freed, 1)
                tt(xT[:, t, :, HP:HALF], xT[:, t, :, HP:HALF], tmp8[:, t, :, :], ALU.add).then_inc(x_updated, 1)
                xup[0] += 1

            dve.memset(ztile, 0.0).then_inc(z_ready, 1)
            dve.memset(csT[:, :, :], 0.0).then_inc(cs_zeroed, 1)
            dve.memset(rw[:, :, :], 0.0).then_inc(rw_zeroed, 1)
            for i in range(5):
                g = flat(grp(("x", i)))
                n = P if i < 4 else NS
                src = g.rearrange("p (t n) -> p t n", t=DT)[:, :, 0:n]
                if i < 4:
                    dve.tensor_copy(xT[:, :, i // 2, (i % 2) * P:(i % 2) * P + P], src).then_inc(freed, 1)
                else:
                    dve.tensor_copy(xT[:, :, :, HP:HALF], src.rearrange("p t (a b) -> p t a b", a=2)).then_inc(freed, 1)
                dve.wait_ge(freed, seen["dve"])
                dve.sem_inc(x_updated, 1)
            g = flat(grp("cols"))
            dve.tensor_copy(cols[:, :], g[:, 0:N_BIAS + N_GAIN])
            dve.tensor_copy(rbias[:, :], g[:, 512:512 + NE]).then_inc(freed, 1)
            settled("cols")
            fill(4)
            turn_up_to(4)

            norm(0, 0, G_MIX)
            dve.wait_ge(s_tab2, 16)

            def rotate(n, h, out, ready):
                if n == "k":
                    dve.wait_ge(q_ready, h + 1)
                elif h:
                    dve.wait_ge(k_ready, h)
                g0 = grp((n, h, 0))
                tt(rt[0], xw(g0), cosr, ALU.mult)
                tt(rt[2], xw(g0), sinr, ALU.mult).then_inc(freed, 1)
                g1 = grp((n, h, 1))
                tt(rt[1], xw(g1), sinr, ALU.mult)
                tt(rt[3], xw(g1), cosr, ALU.mult).then_inc(freed, 1)
                settled("rt")
                for t, (a, b, op) in enumerate(((0, 1, ALU.subtract), (2, 3, ALU.add))):
                    tt(two(out[:, t, 0:NP]), rt[a][:, :, 0:HP], rt[b][:, :, 0:HP], op)
                    last = tt(two(out[:, t, NP:T]), rt[a][:, :, HP:HALF], rt[b][:, :, HP:HALF], op)
                last.then_inc(ready, 1)

            rotate("q", 0, qT, q_ready)
            rotate("k", 0, kT, k_ready)
            for h in range(RH):
                fill()
                g = flat(grp(("ks", h)))
                dve.tensor_copy(ks[0:NS, :], g[0:NS, 0:RD]).then_inc(freed, 1)
                settled("ks")
                dve.wait_ge(k_ready, h + 1)
                tt(kmask[0:NS, :, :], wide(ks[0:NS, :].unsqueeze(1), [NS, NS, RD]),
                   wide(ident[0:NS, 0:NS].unsqueeze(2), [NS, NS, RD]), ALU.mult).then_inc(km_ready, 1)
                for pr, js in (("sa", (0, 1)), ("sb", (2, 3))):
                    g = grp((pr, h))
                    for b, j in enumerate(js):
                        last = tt(PT[j], g[:, b, 0:NP - P * j], decay[:, h, 0:NP - P * j], ALU.mult)
                    last.then_inc(freed, 1)
                fill()
                g = grp(("o", h))
                dve.tensor_copy(oT[:, :, 0:NP], g).then_inc(freed, 1)
                name = ("S", h)
                slot = load_no[name] % 6
                S = W[:, slot, :].rearrange("p (b n) -> p b n", b=NS)
                dve.wait_ge(slot_in[slot], landed[name])
                for b2 in range(4):
                    g = grp(("kv", h, b2))
                    for b in range(2):
                        last = stt(S[:, 2 * b2 + b, :], S[:, 2 * b2 + b, :], float(np.float32(1 - 2.0 ** (-5 - h))),
                                   g[:, b, :], ALU.mult, ALU.add)
                    last.then_inc(freed, 1)
                settled("S")
                dve.sem_inc(st_updated, 1)
                fill()
                fill()
                g = flat(grp(("ot", h)))
                ts(oT[:, :, NP:T], g[:, 0:512].rearrange("p (t b r) -> p t b r", t=2, r=32)[:, :, :, 0], RD ** -0.5,
                   None, ALU.mult).then_inc(freed, 1)
                settled("o")
                dve.sem_inc(o_ready, 1)
                g = grp(("mu", h))
                for t in range(2):
                    last = tt(two(oT[:, t, :]), two(oT[:, t, :]), xw(g), ALU.subtract)
                last.then_inc(freed, 1)
                settled("oc")
                dve.sem_inc(oc_ready, 1)
                fill(2)
                act_took(("var", h))
                link(dve.reciprocal(rs2, rs2))
                r = rs2.rearrange("p a b -> p (a b)")
                for t in range(2):
                    last = tt(oT[:, t, :], oT[:, t, :], r, ALU.mult)
                link(last)
                act_took(("g", h, 1))
                for t in range(2):
                    gn = cols[:, N_BIAS + G_GN + 2 * h + t:N_BIAS + G_GN + 2 * h + t + 1]
                    stt(yT[:, t, :, 0:HP], two(oT[:, t, 0:NP]), gn, gT[:, t, :, 0:HP], ALU.mult, ALU.mult)
                    last = stt(yT[:, t, :, HP:HALF], two(oT[:, t, NP:T]), gn, gT[:, t, :, HP:HALF],
                               ALU.mult, ALU.mult)
                last.then_inc(y_ready, 1)
                if h + 1 < RH:
                    rotate("q", h + 1, qT, q_ready)
                    rotate("k", h + 1, kT, k_ready)
                for t in range(DT):
                    residual(("y", h, t), t, 16)
            fill(ADA_UNITS)

            def route(l):
                s = L[l]
                v = lambda a: a.rearrange("p a b -> p (a b)")
                b16 = lambda a: wide(a.unsqueeze(1), [P, 5, NE])
                over = lambda a: wide(a.unsqueeze(2), [P, 5, NE])
                over4 = lambda a: wide(a.unsqueeze(2), [P, 5, NG])
                g = flat(grp(("ru", l)))
                part = g[:, 0:5 * P].rearrange("p (i j e) -> p i e j", i=5, j=4)[:, :, 0:NE, :]
                dve.tensor_reduce(R["sc"][:, 0:4, :], part[:, 0:4], AX.X, ALU.add)
                dve.tensor_reduce(R["sc"][0:NS, 4:5, :], part[0:NS, 4:5], AX.X, ALU.add).then_inc(freed, 1)
                settled("logits")
                dve.sem_inc(s["logits_ready"], 1)
                dve.wait_ge(s["scores_ready"], 1)
                link(tt(R["sel"], R["sc"], b16(rbias[:, :]), ALU.add))
                x = v(R["sel"]).rearrange("p (a b) -> p a b", b=2)
                tt(hi, x[:, :, 0], x[:, :, 1], ALU.max)
                link(tt(lo, x[:, :, 0], x[:, :, 1], ALU.min))
                hh, ll = (a.rearrange("p (a b) -> p a b", b=2) for a in (hi, lo))
                top1, m2, l2, gs, e4, c4_, ing, inb = (v(R4[n]) for n in "top1 m2 l2 gs e4 c4 ing inb".split())
                tt(top1, hh[:, :, 0], hh[:, :, 1], ALU.max)
                tt(m2, hh[:, :, 0], hh[:, :, 1], ALU.min)
                link(tt(l2, ll[:, :, 0], ll[:, :, 1], ALU.max))
                link(tt(m2, m2, l2, ALU.max))
                link(tt(gs, top1, m2, ALU.add))
                link(dve.tensor_reduce(R5["v1"], R4["gs"], AX.X, ALU.max))
                link(tt(R4["e4"], R4["gs"], over4(R5["v1"]), ALU.is_equal))
                link(tt(R4["c4"], R4["e4"], wide(cst("rev4").unsqueeze(1), [P, 5, NG]), ALU.mult))
                link(dve.tensor_reduce(R5["m"], R4["c4"], AX.X, ALU.max))
                link(tt(R4["ing"], R4["c4"], over4(R5["m"]), ALU.is_equal))
                link(ts(inb, ing, -1.0, 1e30, ALU.add, ALU.mult))
                q4 = lambda a: v(a).rearrange("p (a b) -> p a b", b=EG)
                w4 = lambda a: wide(a.unsqueeze(2), [P, 20, EG])
                link(tt(q4(R["a"]), q4(R["sel"]), w4(ing), ALU.mult))
                link(tt(q4(R["a"]), q4(R["a"]), w4(inb), ALU.add))
                for n, src in (("oh1", "a"), ("oh2", "b")):
                    link(dve.tensor_reduce(R5["v1"], R[src], AX.X, ALU.max))
                    link(tt(R["t"], R[src], over(R5["v1"]), ALU.is_equal))
                    link(tt(R["t"], R["t"], b16(cst("rev16")), ALU.mult))
                    link(dve.tensor_reduce(R5["m"], R["t"], AX.X, ALU.max))
                    link(tt(R[n], R["t"], over(R5["m"]), ALU.is_equal))
                    if n == "oh1":
                        link(stt(v(R["b"]), v(R["oh1"]), -3e38, v(R["a"]), ALU.mult, ALU.add))
                link(tt(R["M"], R["oh1"], R["oh2"], ALU.add))
                tt(R["M"], R["M"], over(cst("valid")), ALU.mult).then_inc(s["mask_ready"], 1)
                for n, o in (("s1", "oh1"), ("s2", "oh2")):
                    link(tt(R["t"], R["sc"], R[o], ALU.mult))
                    link(dve.tensor_reduce(R5[n], R["t"], AX.X, ALU.add))
                link(tt(R5["dsum"], R5["s1"], R5["s2"], ALU.add))
                link(dve.reciprocal(R5["dsum"], R5["dsum"]))
                tt(R5["w1"], R5["s1"], R5["dsum"], ALU.mult)
                tt(R5["w2"], R5["s2"], R5["dsum"], ALU.mult)

            def place(l):
                s = L[l]
                v = lambda a: a.rearrange("p a b -> p (a b)")
                b16 = lambda a: wide(a.unsqueeze(1), [P, 5, NE])
                g = flat(grp(("cnt", l)))
                dve.tensor_copy(v(R["pos"]), g[:, 0:5 * NE])
                dve.tensor_copy(v(R["t"]), g[:, 512:512 + 5 * NE]).then_inc(freed, 1)
                settled("cnt")
                for i in range(1, 5):
                    link(tt(R["t"][:, i, :], R["t"][:, i, :], R["t"][:, i - 1, :], ALU.add))
                dve.tensor_copy(cnt, R["t"][:, 4, :])
                link(tt(R["pos"][:, 1:5, :], R["pos"][:, 1:5, :], R["t"][:, 0:4, :], ALU.add))
                link(ts(ov, cnt, float(MAIN), None, ALU.is_gt))
                for n in range(2, 5):
                    link(stt(ov, cnt, float(MAIN * n), ov, ALU.is_gt, ALU.add))
                a, b = ov, ova
                for st in (1, 2, 4, 8):
                    dve.tensor_copy(b[:, 0:st], a[:, 0:st])
                    link(tt(b[:, st:NE], a[:, st:NE], a[:, 0:NE - st], ALU.add))
                    a, b = b, (ovb if b is ova else ova)
                run = a
                tt(dlt, run, ov, ALU.subtract)
                link(ts(base16, cst("iota16"), float(P), None, ALU.mult))
                link(tt(dlt, dlt, cst("iota16"), ALU.subtract))
                link(ts(dlt, dlt, float(NE - 1), float(P), ALU.add, ALU.mult))
                link(ts(v(R["t"]), v(R["pos"]), float(MAIN), None, ALU.is_ge))
                link(tt(R["t"], R["t"], b16(dlt), ALU.mult))
                link(tt(R["slot"], R["pos"], b16(base16), ALU.add))
                link(tt(R["slot"], R["slot"], R["t"], ALU.add))
                for j, o in enumerate(("oh1", "oh2")):
                    link(tt(R["t"], R["slot"], R[o], ALU.mult))
                    link(dve.tensor_reduce(R5["m"], R["t"], AX.X, ALU.add))
                    link(dve.tensor_copy(didx[:, j, :], R5["m"]))
                link(tt(cmp8[0:1], wide(run[0:1].unsqueeze(1), [1, 8, NE]),
                        wide(cst("iota8")[0:1].unsqueeze(2), [1, 8, NE]), ALU.is_le))
                link(dve.tensor_reduce(nb8[0:1, :], cmp8[0:1], AX.X, ALU.add))
                ts(bex[0:1, NE:MAXBLK], nb8[0:1, :], float(NE - 1), None, ALU.min)
                dve.tensor_copy(bex[0:1, 0:NE], cst("iota16")[0:1, :])
                link(ts(nit[0:1, 0:1], run[0:1, NE - 1:NE], 0.0, float(NE // 2 - 1), ALU.is_gt, ALU.add))
                for n in (2, 4, 6):
                    link(stt(nit[0:1, 0:1], run[0:1, NE - 1:NE], float(n), nit[0:1, 0:1], ALU.is_gt, ALU.add))
                link(dve.tensor_copy(bexp[0:1, :], bex[0:1, :]))
                dve.tensor_copy(niter[0:1, 0:1], nit[0:1, 0:1]).then_inc(s["route_ready"], 1)

            def moe(l):
                s = L[l]
                if l == 0:
                    dve.wait_ge(z_out, 16 * 2 * (MAXBLK - NE))
                    dve.wait_ge(st_out, 16 * RH)
                dve.memset(R["sc"].rearrange("p a b -> p (a b)"), 0.5).then_inc(s["sc_filled"], 1)
                dve.memset(tabz, 0.0).then_inc(s["tab_zero"], 1)
                norm(1 + 3 * l, 48 * l + 24, G_FFN + 8 * l)
                for f in range(FT):
                    if f == 0:
                        route(l)
                    if f == 1:
                        place(l)
                    if f == 3:
                        g = flat(grp(("ix", l)))
                        dve.tensor_copy(idx[:, :], g[:, 0:TABLE]).then_inc(freed, 1)
                    g = grp(("su", l, f))
                    act_took(("sg", l, f))
                    tt(shT[:, f, :, :], xw(g), sgs, ALU.mult).then_inc(freed, 1)
                    settled("sh")
                    dve.sem_inc(s["shT_ready"], 1)
                psX = PS[:, 4, :]

                def block_of(b):
                    dve.wait_ge(s["sg_ready"], b + 1)
                    dve.wait_ge(s["w_used"], b * 3 + 3)
                    tt(hid, sg, PS[:, 3, :], ALU.mult).then_inc(s["hid_ready"], 1)
                    dve.wait_ge(s["ht_done"], b + 1)
                    dve.wait_ge(s["w_used"], b * 3 + 2)
                    dve.tensor_copy(hidT.rearrange("p a b -> p (a b)"), psX).then_inc(s["hidT_ready"], 1)

                block_of(0)
                dve.wait_ge(s["route_ready"], 1)
                turns = dve.value_load(niter[0:1, 0:1], min_val=NE // 2 - 1, max_val=MAXBLK // 2 - 1)
                with dve.Fori(0, turns) as it:
                    block_of(it * 2 + 1)
                    block_of(it * 2 + 2)
                block_of(turns * 2 + 1)
                dve.wait_ge(s["w_used"], turns * 6 + 7)
                gate = 48 * l + 40

                def combine(i):
                    n = P if i < 4 else NS
                    dve.wait_ge(s["first_weighted"], i + 1)
                    dve.wait_ge(s["got"][2 * i + 1], 16)
                    out = hbT[i % 2].rearrange("p t n -> p (t n)")
                    stt(out[0:n, :], y_pair(l, i)[1][0:n, :], R5["w2"][0:n, i:i + 1], out[0:n, :],
                        ALU.mult, ALU.add).then_inc(s["comb_ready"], 1)

                for t in range(DT):
                    residual(("sd", l, t), t, gate)
                    if t in (4, 6):
                        combine(t // 2 - 2)
                dve.wait_ge(x_updated, xup[0])
                for i in range(5):
                    add_back(l, i, gate)
                    if i + 2 < 5:
                        combine(i + 2)

            def add_back(l, i, gate):
                g = flat(grp(("cb", l, i)))
                src = g.rearrange("p (t n) -> p t n", t=DT)
                if i < 4:
                    for t in range(DT):
                        xs = xT[:, t, i // 2, (i % 2) * P:(i % 2) * P + P]
                        last = stt(xs, src[:, t, :], mod[:, gate + t, 0:1], xs, ALU.mult, ALU.add)
                    last.then_inc(freed, 1)
                else:
                    t8 = sg[:, 0:DT * NS].rearrange("p (t n) -> p t n", t=DT)
                    link(tt(t8, src[:, :, 0:NS], mod[:, gate:gate + DT, 1:NSEQ], ALU.mult))
                    xs = xT[:, :, :, HP:HALF]
                    tt(xs, xs, t8.rearrange("p t (a b) -> p t a b", a=2), ALU.add).then_inc(freed, 1)
                settled("x")
                dve.sem_inc(x_updated, 1)
                xup[0] += 1

            moe(0)

            norm(2, 96, G_KV)
            act_took("zk")
            g = grp("kr")
            tt(mt[0][0:ROPE], xw(g)[0:ROPE], sinm[0:ROPE], ALU.mult).then_inc(freed, 1)
            link(tt(mt[1][0:ROPE], zk[0:ROPE], cosm[0:ROPE], ALU.mult))
            tt(two(kpeT[0:ROPE, 0:NP]), mt[1][0:ROPE, :, 0:HP], mt[0][0:ROPE, :, 0:HP], ALU.add)
            tt(two(kpeT[0:ROPE, NP:T]), mt[1][0:ROPE, :, HP:HALF], mt[0][0:ROPE, :, HP:HALF],
               ALU.add).then_inc(kpe_ready, 1)
            norm(3, 48, G_MIX + 8, same_x=True)
            act_took("zss")
            link(dve.reciprocal(rl, rl))
            for t in range(2):
                gc = cols[:, N_BIAS + G_CKV + t:N_BIAS + G_CKV + t + 1]
                stt(two(ckvT[:, t, 0:NP]), zT[:, t, :, 0:HP], gc, rl[:, :, 0:HP], ALU.mult, ALU.mult)
                last = stt(two(ckvT[:, t, NP:T]), zT[:, t, :, HP:HALF], gc, rl[:, :, HP:HALF], ALU.mult, ALU.mult)
            last.then_inc(ckv_ready, 1)
            dve.memset(qsl.rearrange("p a b c -> p (a b c)"), 0.0)

            act_took("qss")
            link(dve.reciprocal(rl, rl))
            for t in range(2):
                gc = cols[:, N_BIAS + G_CQ + t:N_BIAS + G_CQ + t + 1]
                last = stt(cqT[:, t, :, :], zT[:, t, :, :], gc, rl, ALU.mult, ALU.mult)
            last.then_inc(cq_ready, 1)

            def query(h):
                for t in range(2):
                    g = grp(("ql", h, t))
                    dve.tensor_copy(two(ql[:, t, 0:NP]), g[:, :, 0:HP])
                    last = dve.tensor_copy(smp(qsl[:, t, :, h]), g[:, :, HP:HALF])
                    last.then_inc(freed, 1)
                settled("ql")
                dve.sem_inc(ql_ready, 1)
                g = grp(("qr", h))
                tt(qt[0][0:ROPE], xw(g)[0:ROPE], sinm[0:ROPE], ALU.mult).then_inc(freed, 1)
                link(tt(qt[1][0:ROPE], qpr[0:ROPE], cosm[0:ROPE], ALU.mult))
                settled("qr")
                tt(two(qpe[0:ROPE, 0:NP]), qt[1][0:ROPE, :, 0:HP], qt[0][0:ROPE, :, 0:HP], ALU.add)
                tt(smp(qsl[0:ROPE, 2, :, h]), qt[1][0:ROPE, :, HP:HALF], qt[0][0:ROPE, :, HP:HALF],
                   ALU.add).then_inc(qpe_ready, 1)

            query(0)
            for h in range(MH):
                for name, chunks in SCORES:
                    n = group_no[(name, h)]
                    dve.wait_ge(group_done, n + 1)
                    g = flat(pair(n))
                    for i, at in chunks:
                        d = g[:, at + i * P:at + (i + 1) * P]
                        last = tt(d, d, cst("causal"), ALU.add)
                    link(last)
                    for i, at in chunks:
                        last = dve.tensor_reduce(mcol[:, i:i + 1], g[:, at:at + (i + 1) * P], AX.X, ALU.max)
                link(last)
                ts(mcol[:, 4:8], mcol[:, 0:4], -MLA_SCALE, None, ALU.mult).then_inc(mx_ready, 1)
                act_took(("sb_mla", h))
                link(dve.reciprocal(mcol[:, 12:16], mcol[:, 8:12]))
                for i in range(4):
                    c = pr_[:, TRI[i]:TRI[i + 1]]
                    last = ts(c, c, mcol[:, 12 + i:13 + i], None, ALU.mult)
                last.then_inc(p_ready, 1)
                if h + 1 < MH:
                    act_took(("qp", h + 1))
                    query(h + 1)
                g = grp(("ol", h))
                dve.tensor_copy(olat, g).then_inc(freed, 1)

            def scan(b):
                q, j = b // 4, b % 4
                for t in (0, 2):
                    m = P if t < 2 else ROPE
                    g = flat(grp(("kt3", b, t)))
                    dve.tensor_copy(KT[0:m, t, :], g[0:m, :]).then_inc(freed, 1)
                g = flat(grp(("sp", b)))
                for c in range(4):
                    last = dve.tensor_copy(S_sb[q][32 * j:32 * j + 32, c * 256:(c + 1) * 256],
                                           g[32 * c:32 * c + 32, 0:256])
                last.then_inc(freed, 1)

            def softmax(q):
                new = lambda a: wide(a[:, NP + 4 * q:NP + 4 * q + 4].unsqueeze(2), [a.shape[0], 4, 32])
                for t in range(3):
                    m, k = (P, ckvT[:, t, :]) if t < 2 else (ROPE, kpeT[0:ROPE, :])
                    last = tt(prodn[0:m, t, :].rearrange("p (a b) -> p a b", a=4), qsl[0:m, t, 4 * q:4 * q + 4, :],
                              new(k), ALU.mult)
                last.then_inc(prodn_ready, 1)
                g = flat(grp(("sn", q)))
                dve.tensor_copy(S_sb[q][:, PAST:PAST + 1], g[:, 0:1]).then_inc(freed, 1)
                settled("S")
                link(dve.tensor_reduce(mcol2[:, 0:1], S_sb[q], AX.X, ALU.max))
                ts(mcol2[:, 1:2], mcol2[:, 0:1], -MLA_SCALE, None, ALU.mult).then_inc(smx_ready, 1)
                dve.wait_ge(se_ready, q + 1)
                link(dve.reciprocal(mcol2[:, 3:4], mcol2[:, 2:3]))
                ts(Ps, Ps, mcol2[:, 3:4], None, ALU.mult).then_inc(sp_ready, 1)

            def attend(q):
                g = grp(("pv", q))
                dve.wait_ge(sp_ready, q + 1)
                link(ts(onew, g[:, 1, 0:LAT], Ps[:, PAST:PAST + 1], None, ALU.mult))
                tt(olr, g[:, 0, 0:LAT], onew, ALU.add).then_inc(freed, 1)
                settled("olr")
                dve.sem_inc(olr_ready, 1)
                g = flat(grp(("olt", q)))
                for t in range(2):
                    last = dve.tensor_copy(osl[:, t, 4 * q:4 * q + 4, :],
                                           g[:, t * P:(t + 1) * P].rearrange("p (a b) -> p a b", a=4)[:, :, 0:MH])
                last.then_inc(freed, 1)

            for b in range(4):
                scan(b)
            softmax(0)
            scan(4)
            attend(0)
            for b in range(5, NS):
                scan(b)
            softmax(1)
            attend(1)
            for t in range(DT):
                residual(("mo", t), t, 48 + 16)
            moe(1)
            norm(5, 0, G_FIN, modulated=False)

        def page_loop(eng, b, w, cache, at, width, landed_sem, first=0, count=NPAGE):
            with eng.Fori(0, count) as pg:
                page = eng.value_load(ptab[0:1, bass.ds(pg + (b * NPAGE + first), 1)], min_val=0,
                                      max_val=A[cache].shape[0] - 1)
                eng.dma_start(w[:, bass.ds(pg * (LAT + ROPE) + at, width)],
                              A[cache][bass.ds(page, 1)].rearrange("a p c -> p (a c)")).then_inc(landed_sem, 16)

        def load_pages(eng, b, slot, cache, at, width, landed_sem, tail_sem):
            page_loop(eng, b, W[:, slot, :], cache, at, width, landed_sem)
            if b in TAILS:
                page_loop(eng, TAIL_SEQ, W[:, slot, :], cache, NPAGE * (LAT + ROPE) + at, width, tail_sem,
                          TAILS.index(b) * TAIL_PAGES, TAIL_PAGES)

        @block.gpsimd
        def _(pool):
            def moe(l):
                s = L[l]
                pool.wait_ge(s["tab_zero"], 1)
                pool.dma_start(t_dram[l].rearrange("(a b) c -> a (b c)", b=P), tabz[0:TABLE, :]).then_inc(s["tab_zeroed"], 16)
                pool.wait_ge(s["tab_zeroed"], 16)
                pool.wait_ge(s["route_ready"], 1)
                for i in range(5):
                    n = P if i < 4 else NS
                    for j in range(2):
                        pool.indirect_dma_start(
                            out=t_dram[l], out_offset=bass.IndirectOffsetOnAxis(ap=didx[0:n, j, i:i + 1], axis=0),
                            in_=cst("tokid")[0:n, i:i + 1], in_offset=None).then_inc(s["scattered"], 16)
                pool.wait_ge(s["scattered"], 160)
                pool.dma_start(tabr[0:TABLE, :], t_dram[l].rearrange("(a b) c -> a (b c)", b=P)).then_inc(s["tab_in"], 16)
                n_ix, c_ix = group_who[group_no[("ix", l)]]
                pool.wait_ge(took[n_ix], c_ix)
                pool.wait_ge(s["rows_out"][0], 48)
                pool.wait_ge(s["rows_out"][1], 32)

                def gather(b, u, nth):
                    pool.tensor_copy(idxc[:, u:u + 1], idx[:, b:b + 1] if isinstance(b, int) else
                                     idx[:, bass.ds(b, 1)]).then_inc(s["idxc_ready"], 1)
                    pool.wait_ge(s["idxc_ready"], nth)
                    pool.sem_inc(s["idxc_seen"], 1)
                    pool.indirect_dma_start(
                        out=hblk[u], out_offset=None, in_=h_dram[l],
                        in_offset=bass.IndirectOffsetOnAxis(ap=idxc[:, u:u + 1], axis=0)).then_inc(s["gathered"][u], 16)

                def store(b, u, need):
                    pool.wait_ge(s["yout_ready"], need)
                    rows = y_dram.rearrange("(b p) d -> b p d", p=P)
                    dst = rows[b] if isinstance(b, int) else rows[bass.ds(b, 1)].rearrange("a p d -> p (a d)")
                    pool.dma_start(dst, ysb[u]).then_inc(s["stored"][u], 16)

                gather(0, 0, 1)
                gather(1, 1, 2)
                turns = pool.value_load(niter[0:1, 0:1], min_val=NE // 2 - 1, max_val=MAXBLK // 2 - 1)

                def turn(b, nth):
                    for u in range(2):
                        pool.wait_ge(s["th_done"], b + (u + 1))
                        pool.wait_ge(s["gathered"][u], nth * 16 + 16)
                        gather(b + (u + 2), u, b + (u + 3))
                        store(b + u, u, b + (u + 1))

                turn(0, 0)
                with pool.Fori(0, turns) as it:
                    turn(it * 2 + 2, it + 1)
                for u in range(2):
                    pool.wait_ge(s["gathered"][u], turns * 16 + 32)
                    pool.wait_ge(s["stored"][u], turns * 16 + 16)
                pool.wait_ge(s["w_used"], turns * 6 + 7)
                pool.sem_inc(s["idxc_seen"], 1)
                for i in range(5):
                    n = P if i < 4 else NS
                    for j in range(2):
                        pool.indirect_dma_start(
                            out=y_pair(l, i)[j][0:n, :], out_offset=None, in_=y_dram,
                            in_offset=bass.IndirectOffsetOnAxis(ap=didx[0:n, j, i:i + 1], axis=0)
                        ).then_inc(s["got"][2 * i + j], 16)

            pool.wait_ge(z_ready, 1)
            pool.wait_ge(h_ready, 2 * DT)
            for b in range(NE, MAXBLK):
                for c in range(2):
                    pool.dma_start(y_dram[b * P:(b + 1) * P, c * 512:(c + 1) * 512], ztile).then_inc(z_out, 16)
            pool.wait_ge(z_out, 16 * 2 * (MAXBLK - NE))
            moe(0)
            pool.wait_ge(s_pt, 16)
            for b in range(NS):
                if b != TAIL_SEQ:
                    k = load_no[("pages", b)]
                    pool.wait_ge(group_done, last_group[k - 6])
                    load_pages(pool, b, k % 6, "cache_kpe", LAT, ROPE, kpe_in[b], kpe_in[TAIL_SEQ])
            moe(1)

        @block.sync
        def _(sp):
            sp.dma_start(rbrow[0:1, :], A["router_bias"].rearrange("(a e) -> a e", a=1)).then_inc(s_rb, 16)
            sp.dma_start(ptab[0:1, :], A["page_table"].rearrange("(x a) b -> x (a b)", x=1)).then_inc(s_pt, 16)

            def experts(l):
                s = L[l]
                base = s["base"]
                srcs = (A["moe_w_gate"][l], A["moe_w_up"][l], A["moe_w_down"][l])

                def fetch(e, u, j):
                    w = W[:, (base + 3 * u + j) % 6, :].rearrange("p (t n) -> p t n", n=(FE, FE, D)[j])
                    src = srcs[j][e] if isinstance(e, int) else srcs[j][bass.ds(e, 1)].rearrange("a k n -> (a k) n")
                    sp.dma_start(w, src.rearrange("(t p) n -> p t n", p=P)).then_inc(s["w_in"][3 * u + j], 16)

                for e, j in ((0, 0), (0, 1), (1, 0), (0, 2), (1, 1)):
                    free_slot(s["prior"] + 3 * e + j)
                    fetch(e, e, j)
                free_slot(s["prior"] + 5)
                sp.wait_ge(s["route_ready"], 1)
                turns = sp.value_load(niter[0:1, 0:1], min_val=NE // 2 - 1, max_val=MAXBLK // 2 - 1)

                def expert_of(b):
                    return sp.value_load(bexp[0:1, bass.ds(b, 1)], min_val=0, max_val=NE - 1)

                sp.wait_ge(s["w_used"], 2)
                with sp.Fori(0, turns) as it:
                    for u in range(2):
                        b = it * 2 + (2 + u)
                        before, e = expert_of(b - 1), expert_of(b)
                        sp.wait_ge(s["w_used"], b * 3 - 5)
                        fetch(e, u, 0)
                        sp.wait_ge(s["w_used"], b * 3 - 4)
                        fetch(before, 1 - u, 2)
                        sp.wait_ge(s["w_used"], b * 3 - 3)
                        fetch(e, u, 1)
                sp.wait_ge(s["w_used"], turns * 6 + 2)
                fetch(expert_of(turns * 2 + 1), 1, 2)

            def free_slot(k):
                if k < 6 or (k - 6) < expert_floor[0]:
                    return
                name = loads[k - 6][0]
                sp.wait_ge(group_done, last_group[k - 6])
                if name[0] == "S":
                    sp.wait_ge(ss_out[name[1]], 32)

            expert_floor = [0]
            done_moe = 0
            for k, (name, slot, parts) in enumerate(loads):
                if done_moe < 2 and k == L[done_moe]["prior"]:
                    experts(done_moe)
                    done_moe += 1
                    expert_floor[0] = k
                free_slot(k)
                if k == L[0]["prior"] + 1:
                    sp.wait_ge(L[0]["comb_ready"], 5)
                if k == 0:
                    sp.dma_start(xrows[:, 0:4, :], A["x_prompt"][0].rearrange("(i p) d -> p i d", p=P)).then_inc(s_x, 16)
                    sp.dma_start(xrows[0:NS, 4, :], A["x_sample"].rearrange("b a d -> (b a) d")).then_inc(s_x, 16)
                if k == 1:
                    sp.wait_ge(s_rows, 16 * 9)
                if k == 6:
                    sp.wait_ge(rw_zeroed, 1)
                    sp.dma_start(rw[:, :, 0:NE], A["router_w"].rearrange("(t p) e -> p t e", p=P)).then_inc(s_rw, 16)
                if k == 5:
                    sp.dma_start(C[:, FIRST:CW], A["tables"][:, FIRST:CW]).then_inc(s_tab2, 16)
                w = W[:, slot, :]
                if parts is not None:
                    for dst, src in parts:
                        sp.dma_start(dst(w), src).then_inc(slot_in[slot], 16)
                else:
                    b = name[1]
                    if b == 0:
                        sp.wait_ge(s_pt, 16)
                    load_pages(sp, b, slot, "cache_ckv", 0, LAT, slot_in[slot], slot_in[slot])
            while done_moe < 2:
                experts(done_moe)
                done_moe += 1


_INS = ["x_prompt", "x_sample", "c_prompt", "c_sample", "state_ret", "cache_ckv", "cache_kpe", "page_table",
        "w_ada", "b_ada", "norm_mix_g", "norm_ffn_g", "ret_w_in", "ret_gn_g", "ret_w_out", "kv_w_ada", "kv_b_ada",
        "kv_norm_g", "mla_w_dkv", "mla_kv_norm_g", "mla_w_uk", "mla_w_uv", "mla_w_dq", "mla_q_norm_g", "mla_w_uq",
        "mla_w_o", "router_w", "router_bias", "moe_w_gate", "moe_w_up", "moe_w_down", "shared_w_gate",
        "shared_w_up", "shared_w_down", "final_norm_g"]
_OUTS = [("y_p", (1, NP, D)), ("y_s", (NS, 1, D)), ("state_p", (1, 1, RH, RD, RD)), ("state_s", (1, NS, RH, RD, RD)),
         ("ckv_p", (1, NP, LAT)), ("kpe_p", (1, NP, ROPE)), ("ckv_s", (NS, 1, LAT)), ("kpe_s", (NS, 1, ROPE))]


def kernel(**inputs):
    import concourse.bacc as _bacc
    from concourse.bass_utils import run_bass_kernel_spmd as _run

    nc = _bacc.Bacc("TRN2", target_bir_lowering=False, num_devices=1)
    arrays, ins, outs = {}, {}, {}
    for name in _INS:
        arrays[name] = np.ascontiguousarray(inputs[name])
    arrays["tables"] = shape_tables()
    for name, a in arrays.items():
        ins[name] = nc.dram_tensor(name, a.shape, mybir.dt.from_np(a.dtype), kind="ExternalInput").ap()
    for name, shape in _OUTS:
        outs[name] = nc.dram_tensor("out_" + name, shape, F32, kind="ExternalOutput").ap()
    build(nc, ins, outs)
    r = _run(nc, [arrays], core_ids=[0])
    return tuple(r.results[0]["out_" + name] for name, _ in _OUTS)
```
